# Optimizing a Trainium2 kernel written in Bass

```python
import jax, jax.numpy as jnp
from jax import lax
import numpy as np

D_MODEL = 1024
BATCH = 1
SEQ = 128
DEPTH = 2
DEC_BATCH = 1
DEC_SEQ = 256
PAST_LEN = 128

GRID_W = 64
D_A = D_MODEL
CONV_A_WIDTH = 3
D_B = D_MODEL
CONV_B_WIDTH = 31
HEAD_DIM = 64
N_Q_HEADS = D_MODEL // HEAD_DIM
N_KV_HEADS = N_Q_HEADS // 4
KV_GROUP = N_Q_HEADS // N_KV_HEADS
D_Q = N_Q_HEADS * HEAD_DIM
D_KV = N_KV_HEADS * HEAD_DIM
Q_BLOCK = 128
ROPE_THETA = 10000.0
N_EXPERTS = 16
N_GROUPS = 4
EXPERTS_PER_GROUP = N_EXPERTS // N_GROUPS
TOPK_GROUPS = 1
TOP_K = 2
D_EXPERT = D_MODEL // 2
MOE_BLOCK = 128
N_BRANCHES = 3
SECTION_WIDTHS = (D_A, D_A, D_A, D_B, D_B, D_Q, D_KV, D_KV, N_BRANCHES * D_MODEL)
SPLIT_POINTS = tuple(int(s) for s in np.cumsum(SECTION_WIDTHS)[:-1])
IN_COLS = sum(SECTION_WIDTHS)
N_MOD = 6
DEEPNORM_ALPHA = (2 * DEPTH) ** 0.25
DEEPNORM_BETA = (8 * DEPTH) ** -0.25
LN_EPS = 1e-5
RMS_EPS = 1e-6

kernel_name = 'hybrid_diffusion_prefix_trunk_step'

def layer_norm(x, g, b):
    xf = x.astype(jnp.float32)
    xc = xf - xf.mean(-1, keepdims=True)
    var = (xc * xc).mean(-1, keepdims=True)
    return (xc * lax.rsqrt(var + LN_EPS) * g.astype(jnp.float32) + b.astype(jnp.float32)).astype(x.dtype)

def rms_norm(x, g):
    xf = x.astype(jnp.float32)
    return (xf * lax.rsqrt((xf * xf).mean(-1, keepdims=True) + RMS_EPS) * g.astype(jnp.float32)).astype(x.dtype)

def depthwise_conv(x, w):
    k_width, ch = w.shape
    return lax.conv_general_dilated(
        x, w[:, None, :].astype(x.dtype), window_strides=(1,),
        padding=[(k_width // 2, k_width // 2)],
        dimension_numbers=('NWC', 'WIO', 'NWC'), feature_group_count=ch)

def grid_positions(n_tokens):
    rows = n_tokens // GRID_W
    row = jnp.repeat(jnp.arange(rows, dtype=jnp.int32), GRID_W)
    col = jnp.tile(jnp.arange(GRID_W, dtype=jnp.int32), rows)
    return row, col

def rope_1d(x, pos):
    half = x.shape[-1] // 2
    freqs = jnp.power(ROPE_THETA, -jnp.arange(half, dtype=jnp.float32) / half)
    ang = pos.astype(jnp.float32)[:, None] * freqs[None, :]
    cos = jnp.cos(ang)[:, None, :]
    sin = jnp.sin(ang)[:, None, :]
    xf = x.astype(jnp.float32)
    x1, x2 = xf[..., :half], xf[..., half:]
    return jnp.concatenate([x1 * cos - x2 * sin, x2 * cos + x1 * sin], axis=-1).astype(x.dtype)

def rope_2d(x, row, col):
    half = HEAD_DIM // 2
    return jnp.concatenate([rope_1d(x[..., :half], row), rope_1d(x[..., half:], col)], axis=-1)

def block_attention(q, k, v):
    bsz, sq = q.shape[0], q.shape[1]
    n_blk = sq // Q_BLOCK
    qb = q.reshape(bsz, n_blk, Q_BLOCK, N_KV_HEADS, KV_GROUP, HEAD_DIM).transpose(1, 0, 2, 3, 4, 5)
    scale = HEAD_DIM ** -0.5

    def one_block(q_blk):
        s = jnp.einsum('bqkgd,bskd->bkgqs', q_blk, k).astype(jnp.float32) * scale
        p = jax.nn.softmax(s, axis=-1).astype(v.dtype)
        return jnp.einsum('bkgqs,bskd->bqkgd', p, v)

    o = lax.map(one_block, qb)
    return o.transpose(1, 0, 2, 3, 4, 5).reshape(bsz, sq, D_Q)

def parallel_mixer(h, lp, ctx_k, ctx_v, pos):
    bsz, s, _ = h.shape
    proj = jnp.einsum('bsd,dn->bsn', h, lp['w_in'])
    a_b, a_c, a_x, b_u, b_g, q, k, v, gates = jnp.split(proj, SPLIT_POINTS, axis=-1)
    y_a = jnp.einsum('bsc,cd->bsd', a_b * depthwise_conv(a_c * a_x, lp['conv_a_w']), lp['w_a_out'])
    u = depthwise_conv(b_u * jax.nn.sigmoid(b_g), lp['conv_b_w'])
    u = u + lp['conv_b_b'].astype(u.dtype)
    y_b = jnp.einsum('bsc,cd->bsd', jax.nn.silu(layer_norm(u, lp['norm_b_g'], lp['norm_b_b'])), lp['w_b_out'])
    q = rms_norm(q.reshape(bsz, s, N_Q_HEADS, HEAD_DIM), lp['q_norm_g'])
    k = rms_norm(k.reshape(bsz, s, N_KV_HEADS, HEAD_DIM), lp['k_norm_g'])
    v = v.reshape(bsz, s, N_KV_HEADS, HEAD_DIM)
    if pos is None:
        o = block_attention(q, k, v)
    else:
        row, col = pos
        keys = jnp.concatenate([ctx_k.astype(k.dtype), rope_2d(k, row, col)], axis=1)
        vals = jnp.concatenate([ctx_v.astype(v.dtype), v], axis=1)
        o = block_attention(rope_2d(q, row, col), keys, vals)
    y_c = jnp.einsum('bsc,cd->bsd', o, lp['w_c_out'])
    g_a, g_b, g_c = jnp.split(jax.nn.sigmoid(gates), N_BRANCHES, axis=-1)
    out = jnp.einsum('bsd,de->bse', g_a * y_a + g_b * y_b + g_c * y_c, lp['w_o'])
    return out, k, v

def routed_moe(x2, w_router, router_bias, w_gate_up, w_down):
    t_count, d = x2.shape
    scores = jax.nn.sigmoid(jnp.einsum('td,de->te', x2, w_router).astype(jnp.float32))
    sel = scores + router_bias.astype(jnp.float32)
    group_score = lax.top_k(sel.reshape(t_count, N_GROUPS, EXPERTS_PER_GROUP), 2)[0].sum(-1)
    _, g_idx = lax.top_k(group_score, TOPK_GROUPS)
    group_mask = (jnp.arange(N_GROUPS)[None, None, :] == g_idx[:, :, None]).any(axis=1)
    expert_mask = jnp.repeat(group_mask, EXPERTS_PER_GROUP, axis=1)
    _, e_idx = lax.top_k(jnp.where(expert_mask, sel, -jnp.inf), TOP_K)
    w = jnp.take_along_axis(scores, e_idx, axis=1)
    w = w / w.sum(-1, keepdims=True)
    n_assign = t_count * TOP_K
    flat_e = e_idx.reshape(n_assign)
    order = jnp.argsort(flat_e)
    e_sorted = flat_e[order]
    tok_sorted = (order // TOP_K).astype(jnp.int32)
    counts = jnp.zeros((N_EXPERTS,), jnp.int32).at[flat_e].add(1)
    padded = (counts + MOE_BLOCK - 1) // MOE_BLOCK * MOE_BLOCK
    pad_end = jnp.cumsum(padded)
    pad_start = pad_end - padded
    start = jnp.cumsum(counts) - counts
    dest = pad_start[e_sorted] + (jnp.arange(n_assign, dtype=jnp.int32) - start[e_sorted])
    n_blocks = (n_assign + N_EXPERTS * (MOE_BLOCK - 1) + MOE_BLOCK - 1) // MOE_BLOCK
    slot_tok = jnp.full((n_blocks * MOE_BLOCK,), t_count, jnp.int32).at[dest].set(tok_sorted)
    block_exp = jnp.minimum(
        jnp.searchsorted(pad_end, jnp.arange(n_blocks, dtype=jnp.int32) * MOE_BLOCK, side='right'),
        N_EXPERTS - 1)
    x_pad = jnp.concatenate([x2, jnp.zeros((1, d), x2.dtype)], axis=0)

    def run_block(args):
        toks, e = args
        gu = x_pad[toks] @ w_gate_up[e]
        gate, up = jnp.split(gu, 2, axis=-1)
        return (jax.nn.silu(gate) * up) @ w_down[e]

    y_slots = lax.map(run_block, (slot_tok.reshape(n_blocks, MOE_BLOCK), block_exp))
    y_slots = y_slots.reshape(n_blocks * MOE_BLOCK, d)
    y_assign = jnp.zeros((n_assign, d), y_slots.dtype).at[order].set(y_slots[dest])
    return (y_assign.reshape(t_count, TOP_K, d) * w[..., None].astype(y_slots.dtype)).sum(axis=1)

def trunk_layer(x, cond, lp, w_router, router_bias, ctx_k, ctx_v, pos):
    bsz, s, d = x.shape
    mod = jnp.einsum('bd,dn->bn', jax.nn.silu(cond), lp['w_ada']) + lp['b_ada']
    sh1, sc1, g1, sh2, sc2, g2 = jnp.split(mod[:, None, :], N_MOD, axis=-1)
    h = x * (1.0 + sc1) + sh1
    m, k, v = parallel_mixer(h, lp, ctx_k, ctx_v, pos)
    x = layer_norm(DEEPNORM_ALPHA * x + g1 * m, lp['ln_g'][0], lp['ln_b'][0])
    h = x * (1.0 + sc2) + sh2
    f = routed_moe(h.reshape(bsz * s, d), w_router, router_bias, lp['w_gate_up'], lp['w_down']).reshape(bsz, s, d)
    x = layer_norm(DEEPNORM_ALPHA * x + g2 * f, lp['ln_g'][1], lp['ln_b'][1])
    return x, k, v

def setup_inputs(seed: int = 0) -> dict:
    key = jax.random.key(seed)
    ks = jax.random.split(key, 26)

    def nrm(k, shape, scale):
        return jax.random.normal(k, shape, jnp.float32) * scale

    return {
        'x_prompt': nrm(ks[0], (BATCH, SEQ, D_MODEL), 1.0),
        'x_sample': nrm(ks[1], (DEC_BATCH, DEC_SEQ, D_MODEL), 1.0),
        'c': nrm(ks[2], (DEC_BATCH, D_MODEL), 1.0),
        'c_ctx': nrm(ks[3], (D_MODEL,), 1.0),
        'cache_k': nrm(ks[4], (DEC_BATCH, DEPTH, PAST_LEN, N_KV_HEADS, HEAD_DIM), 1.0),
        'cache_v': nrm(ks[5], (DEC_BATCH, DEPTH, PAST_LEN, N_KV_HEADS, HEAD_DIM), 1.0),
        'w_in': nrm(ks[6], (DEPTH, D_MODEL, IN_COLS), D_MODEL ** -0.5),
        'conv_a_w': nrm(ks[7], (DEPTH, CONV_A_WIDTH, D_A), CONV_A_WIDTH ** -0.5),
        'w_a_out': nrm(ks[8], (DEPTH, D_A, D_MODEL), D_A ** -0.5),
        'conv_b_w': nrm(ks[9], (DEPTH, CONV_B_WIDTH, D_B), CONV_B_WIDTH ** -0.5),
        'conv_b_b': nrm(ks[10], (DEPTH, D_B), 0.02),
        'norm_b_g': 1.0 + nrm(ks[11], (DEPTH, D_B), 0.02),
        'norm_b_b': nrm(ks[12], (DEPTH, D_B), 0.02),
        'w_b_out': nrm(ks[13], (DEPTH, D_B, D_MODEL), D_B ** -0.5),
        'q_norm_g': 1.0 + nrm(ks[14], (DEPTH, HEAD_DIM), 0.02),
        'k_norm_g': 1.0 + nrm(ks[15], (DEPTH, HEAD_DIM), 0.02),
        'w_c_out': nrm(ks[16], (DEPTH, D_Q, D_MODEL), D_Q ** -0.5),
        'w_o': nrm(ks[17], (DEPTH, D_MODEL, D_MODEL), DEEPNORM_BETA * D_MODEL ** -0.5),
        'w_ada': nrm(ks[18], (DEPTH, D_MODEL, N_MOD * D_MODEL), D_MODEL ** -0.5),
        'b_ada': nrm(ks[19], (DEPTH, N_MOD * D_MODEL), 0.02),
        'ln_g': 1.0 + nrm(ks[20], (DEPTH, 2, D_MODEL), 0.02),
        'ln_b': nrm(ks[21], (DEPTH, 2, D_MODEL), 0.02),
        'w_router': nrm(ks[22], (D_MODEL, N_EXPERTS), D_MODEL ** -0.5),
        'router_bias': nrm(ks[23], (N_EXPERTS,), 0.01),
        'w_gate_up': nrm(ks[24], (DEPTH, N_EXPERTS, D_MODEL, 2 * D_EXPERT), D_MODEL ** -0.5),
        'w_down': nrm(ks[25], (DEPTH, N_EXPERTS, D_EXPERT, D_MODEL), DEEPNORM_BETA * D_EXPERT ** -0.5),
    }

def reference(x_prompt, x_sample, c, c_ctx, cache_k, cache_v, w_in, conv_a_w, w_a_out, conv_b_w,
              conv_b_b, norm_b_g, norm_b_b, w_b_out, q_norm_g, k_norm_g, w_c_out, w_o, w_ada, b_ada,
              ln_g, ln_b, w_router, router_bias, w_gate_up, w_down):
    lat_pos = grid_positions(x_sample.shape[1])
    ctx_cond = c_ctx[None, :]
    y_prompt = x_prompt
    y_sample = x_sample
    new_k_layers = []
    new_v_layers = []
    for l in range(DEPTH):
        lp = {
            'w_in': w_in[l], 'conv_a_w': conv_a_w[l], 'w_a_out': w_a_out[l],
            'conv_b_w': conv_b_w[l], 'conv_b_b': conv_b_b[l], 'norm_b_g': norm_b_g[l],
            'norm_b_b': norm_b_b[l], 'w_b_out': w_b_out[l], 'q_norm_g': q_norm_g[l],
            'k_norm_g': k_norm_g[l], 'w_c_out': w_c_out[l], 'w_o': w_o[l], 'w_ada': w_ada[l],
            'b_ada': b_ada[l], 'ln_g': ln_g[l], 'ln_b': ln_b[l], 'w_gate_up': w_gate_up[l],
            'w_down': w_down[l],
        }
        y_prompt, k_l, v_l = trunk_layer(y_prompt, ctx_cond, lp, w_router, router_bias, None, None, None)
        new_k_layers.append(k_l)
        new_v_layers.append(v_l)
        y_sample, _, _ = trunk_layer(y_sample, c, lp, w_router, router_bias,
                                     cache_k[:, l], cache_v[:, l], lat_pos)
    new_k = jnp.stack(new_k_layers, axis=1)
    new_v = jnp.stack(new_v_layers, axis=1)
    return (y_prompt, y_sample, new_k, new_v)


_drawn_inputs = setup_inputs


def setup_inputs(seed=0):
    import zlib

    import numpy as np

    out = dict(_drawn_inputs(seed))
    spreads = {}
    factors = {'conv_b_b': 2.879,
     'norm_b_g': 9.838,
     'norm_b_b': 3.867,
     'q_norm_g': 5.143,
     'k_norm_g': 2.76,
     'cache_v': 2.719}
    for name, (base, spread) in spreads.items():
        noise = np.random.default_rng([zlib.crc32(name.encode()), seed]).standard_normal(out[name].shape)
        drawn = base * np.exp(spread * noise) if base else spread * noise
        out[name] = __import__('jax').numpy.asarray(drawn.astype(out[name].dtype))
    for name, factor in factors.items():
        out[name] = (out[name] * factor).astype(out[name].dtype)
    return out
```

```python
import math
from contextlib import ExitStack

import numpy as np

import concourse.bass as bass
from concourse import mybir

F32 = mybir.dt.float32
F16 = mybir.dt.float16
I32 = mybir.dt.int32
ALU = mybir.AluOpType
ACT = mybir.ActivationFunctionType
AX = mybir.AxisListType

P = 128
BLK = 96
STAGES, SPLITS = 6, 3
PCOL = 256
WSCALE = 64.0
UNSCALE = 1.0 / WSCALE
HEAD = 64
GRID_W = 64
LN_EPS, RMS_EPS = 1e-5, 1e-6

CONVB, CONVA, CONVBB, NBG, NBB, LNG, LNB, BADA, QG, KG, NPAR = 0, 31, 34, 35, 36, 37, 39, 41, 47, 48, 49


def shape_constants():
    ident = np.eye(P, dtype=np.float32)
    mean_of_model = np.full((P, P), 1.0 / 1024, np.float32)
    head_mean = np.kron(np.eye(2), np.full((HEAD, HEAD), 1.0 / HEAD)).astype(np.float32)
    rot = np.zeros((P, P), np.float32)
    for d in range(P):
        if d % 32 < 16:
            rot[d, d + 16] = -1.0
        else:
            rot[d, d - 16] = 1.0
    half = 16
    freqs = np.power(np.float32(10000.0), -np.arange(half, dtype=np.float32) / np.float32(half)).astype(np.float32)
    token = np.arange(256)
    row, col = (token // GRID_W).astype(np.float32), (token % GRID_W).astype(np.float32)
    ang = np.zeros((P, 256), np.float32)
    for d in range(P):
        pos = row if d % 64 < 32 else col
        ang[d] = pos * freqs[d % 16]
    earlier = np.triu(np.ones((P, P), np.float32), 1) / 1024
    iota16 = np.tile(np.arange(16, dtype=np.float32), (P, 1))
    table = np.concatenate(
        [ident, mean_of_model, head_mean, rot.T, earlier, np.cos(ang), np.sin(ang), iota16], axis=1)
    return np.ascontiguousarray(table, np.float32), np.tile(np.arange(768), (P, 1)).astype(np.float16)


def section_panels():
    order = [("ada", j) for j in range(8)]
    for j in range(4):
        order += [("bg", j), ("bu", j)]
    order += [("q", j) for j in range(4)] + [("k", 0), ("v", 0)]
    for j in range(4):
        order += [("ac", j), ("ax", j), ("ab", j)]
    order += [("ada", j) for j in (8, 9, 10)]
    ada = iter(range(11, 24))
    for s in "acb":
        for j in range(4):
            order += [("g" + s, j), ("w" + s, j), ("ada", next(ada))]
    order += [("ada", next(ada))]
    order += [("o", j) for j in range(4)]
    return order


MIX = section_panels()
NMIX = len(MIX)
NEXP = 16
SLOT_STEP = 512
EXPERT_FIRST = (("gate", 0), ("up", 0), ("gate", 1), ("up", 1))
EXPERT_LOOP = (("gate", 0), ("down", 0), ("down", 1), ("up", 0), ("gate", 1), ("up", 1))
EXPERT_LAST = (("down", 0), ("down", 1))
EXPERT_PANELS = NEXP * 6
BANK = dict(gate=0, up=4, down=6)
NPANEL = NMIX + EXPERT_PANELS
COLS = dict(ab=0, ac=1024, ax=2048, bu=3072, bg=4096, q=5120, k=6144, v=6400, ga=6656, gb=7680, gc=8704)
TILES_OF = dict(ada=1, v=3)
ATT0 = MIX.index(("ac", 1))
NBATCH = 12
TILE0 = []
for _kind, _j in MIX:
    TILE0.append(TILE0[-1] + _n if TILE0 else 0)
    _n = TILES_OF.get(_kind, 2)
NTILE = TILE0[-1] + _n
BY_ACT = {"bg", "q", "k", "v", "ac", "ga", "gb", "gc"}
TILE_KIND = [k for k, _j in MIX for _ in range(TILES_OF.get(k, 2))]
NPROJ = 3
GRPS = ((0, slice(0, 128)), (1, slice(128, 384)))


def tiles_freed(upto, act):
    return sum((k in BY_ACT) == act for k in TILE_KIND[:upto])


def act_count(n, i):
    return tiles_freed(TILE0[n] + i + 1, True)


def dve_count(n, i):
    return tiles_freed(TILE0[n] + i + 1, False)


NT_ACT, NT_DVE = tiles_freed(NTILE, True), tiles_freed(NTILE, False)
NSMALL = 27
DVE_STEPS, ACT_STEPS, POOL_STEPS = 255, 8, 308
G_USERS = [MIX.index((k, j)) for k in ("bu", "wa", "wc", "wb") for j in range(4)]
POOL_CHUNKS = 5
_beside = [(MIX.index(("q", 0)) + i, 7) for i in range(6)] + [(MIX.index(("ga", 0)) + i, 4) for i in range(13)]
_taps = [(ch, t) for ch in range(POOL_CHUNKS, 8) for t in range(31)]
CONV_TAPS = {}
for _n, _k in _beside:
    CONV_TAPS[_n], _taps = _taps[:_k], _taps[_k:]
assert not _taps
LNB_AT = MIX.index(("wc", 1))


def build(nc, x_prompt, x_sample, c, c_ctx, cache_k, cache_v, w_in, conv_a_w, w_a_out, conv_b_w, conv_b_b,
          norm_b_g, norm_b_b, w_b_out, q_norm_g, k_norm_g, w_c_out, w_o, w_ada, b_ada, ln_g, ln_b,
          w_router, router_bias, w_gate_up, w_down, table, iota, y_prompt, y_sample, new_k, new_v):
    DEPTH = w_in.shape[0]
    ALPHA = float((2 * DEPTH) ** 0.25)
    ctx = ExitStack()
    with ctx:
        def sb(name, shape, dt=F32):
            return ctx.enter_context(nc.sbuf_tensor(name, shape, dt))

        def sem(name):
            return ctx.enter_context(nc.semaphore(name))

        stage = sb("stage", [P, STAGES, 2048])
        split = sb("split", [P, SPLITS, 2, 2048], F16)
        arena = sb("arena", [P, 31336])
        tab = sb("tab", [P, 5 * 128 + 512 + 16])
        ident, mean_mat, head_mat, rot_mat, earlier_mat = (tab[:, 128 * i:128 * i + 128] for i in range(5))
        cos_t, sin_t, iota16 = tab[:, 640:896], tab[:, 896:1152], tab[:, 1152:1168]
        params = sb("params", [P, DEPTH, 8 * NPAR])
        cur = sb("cur", [P, 8, NPAR])
        mod = sb("mod", [P, 6, 8, 2])
        cond_split = sb("cond_split", [P, 2, 8, 2], F16)
        wr = sb("wr", [P, 8, 16])
        rbias = sb("rbias", [P, 16])
        qg8 = sb("qg8", [P, 1])
        eps = sb("eps", [P, 3])
        std = sb("std", [P, 400])
        mx = sb("mx", [P, 48])
        rsum = sb("rsum", [P, 2, 48])
        slots_i = sb("slots_i", [1, 16], I32)
        PS = ctx.enter_context(nc.psum_tensor("PS", [P, 8, 512], F32))

        def region(at, *dims, dt=F32):
            n = math.prod(dims)
            words = n if dt == F32 else n // 2
            v = arena[:, at:at + words]
            if dt != F32:
                v = v.bitcast(dt)
            if len(dims) == 2:
                v = v.rearrange("p (a b) -> p a b", a=dims[0])
            if len(dims) == 3:
                v = v.rearrange("p (a b c) -> p a b c", a=dims[0], b=dims[1])
            return v

        X = region(0, 8, 384)
        H = region(3072, 2, 8, 384, dt=F16)
        BIN = region(6144, 8, 429)
        OPB = region(6144, 2, 8, 384, dt=F16)
        BACC = region(9576, 8, 399)
        OPA = region(12768, 2, 8, 384, dt=F16)
        Q = region(15840, 8, 384)
        SQB = region(15840, 8, 399)
        OPM = region(15840, 2, 8, 384, dt=F16)
        HF = region(19032, 8, 384)
        SQQ = region(19032, 8, 384)
        OPC = region(19032, 2, 8, 384, dt=F16)
        KC = region(22104, 256)
        SQK = region(22360, 2, 384)
        RT = region(23128, 2, 384)
        ROT = region(23896, 2, 256)
        PR = region(22104, 4, 384)
        PT = region(23640, 3, 4, 128)
        M = region(22104, 8, 384)
        KT = region(25176, 2, 512)
        KTS = region(26200, 2, 512)
        V = region(27224, 4, 256)
        AIN = region(28248, 2, 387)
        ACV = region(29024, 2, 385)
        G = region(29800, 2, 384)
        KOUT = region(29800, 256)
        Y = region(30568, 2, 384)
        H2 = region(3072, 8, 384)
        SQ = region(3072, 8, 384)
        GT = region(3072, 2, 512)
        HID = region(4096, 2, 4, 512, dt=F16)
        HTOK = region(6144, 2, 3, 1024, dt=F16)
        XG = region(9216, 2, 8, 896, dt=F16)
        YS = region(9216, 6, 1024)
        YT = region(16384, 8, 896)
        ONE = region(23552, 3, 768, dt=F16)
        GW = region(24704, 3, 768)
        SW = region(27008, 6, 384)
        SIG = region(29800, 2, 2, BLK)
        HF2 = region(6144, 2, BLK)
        sel_at = [30312]

        def small(*dims):
            n = math.prod(dims)
            sel_at[0] += n
            return region(sel_at[0] - n, *dims)
        LG = region(29800, 384)[0:16]
        score, sel, selm, one1, one2, picked, key = (small(3, 16) for _ in range(7))
        pair_hi, pair_lo, grp = small(2, 3, 4), small(2, 3, 4), small(4, 3, 4)
        top = small(3)
        scan = small(4, 16)
        slot = small(3, 16)
        pick_s, pick_w = small(2, 3), small(2, 3)
        gw_tmp = region(16384, 3, 768)
        iota768 = region(18688, 768, dt=F16)
        cond = region(16384, 3, 16)
        PROWS = region(6144, 1024)
        XTOK = region(12768, 3, 1024)
        OUT = region(12768, 3, 1024)

        landed = [sem(f"landed{i}") for i in range(STAGES)]
        hi_done = sem("hi_done")
        lo_done = sem("lo_done")
        panel_used = sem("panel_used")
        small_in = sem("small_in")
        pro_full, pro_free_act, pro_free_dve = sem("pro_full"), sem("pro_free_act"), sem("pro_free_dve")
        cond_sig, cond_ok = sem("cond_sig"), sem("cond_ok")
        tile_full, tile_act, tile_dve = sem("tile_full"), sem("tile_act"), sem("tile_dve")
        cur_ok, eps_ok = sem("cur_ok"), sem("eps_ok")
        h_f, h_hi, h_lo = sem("h_f"), sem("h_hi"), sem("h_lo")
        pads = sem("pads")
        conv_b, conv_dve = sem("conv_b"), sem("conv_dve")
        kv_in, iota_in = sem("kv_in"), sem("iota_in")
        sq_qk = sem("sq_qk")
        ck_full, ck_ok, kn_full, kn_ok, kv_out = (sem("ck_full"), sem("ck_ok"), sem("kn_full"), sem("kn_ok"),
                                                  sem("kv_out"))
        rms_full, rms_std, qk_norm = sem("rms_full"), sem("rms_std"), sem("qk_norm")
        rope_full, rope_ok, swap_ok = sem("rope_full"), sem("rope_ok"), sem("swap_ok")
        s_full, s_max, p_exp, p_norm = sem("s_full"), sem("s_max"), sem("p_exp"), sem("p_norm")
        pt_full, pt_act, pt_dve = sem("pt_full"), sem("pt_act"), sem("pt_dve")
        o_full, o_hi, o_lo = sem("o_full"), sem("o_hi"), sem("o_lo")
        opa_hi, opa_lo = sem("opa_hi"), sem("opa_lo")
        sqb, lnb_full, lnb_msq, lnb_var, lnb_std, lnb_norm, lnb_aff = (
            sem("sqb"), sem("lnb_full"), sem("lnb_msq"), sem("lnb_var"), sem("lnb_std"), sem("lnb_norm"),
            sem("lnb_aff"))
        opb_f, opb_hi, opb_lo = sem("opb_f"), sem("opb_hi"), sem("opb_lo")
        m_ok, opm_hi, opm_lo = sem("m_ok"), sem("opm_hi"), sem("opm_lo")
        z_ok = sem("z_ok")
        z_sq, ln_full, ln_msq, ln_var, ln_std, ln_norm, x_ok = (
            sem("z_sq"), sem("ln_full"), sem("ln_msq"), sem("ln_var"), sem("ln_std"), sem("ln_norm"), sem("x_ok"))
        h2_ok = sem("h2_ok")
        lg_full, lg_ok, lt_full, score_ok = sem("lg_full"), sem("lg_ok"), sem("lt_full"), sem("score_ok")
        ht_full, ht_hi, ht_lo = sem("ht_full"), sem("ht_hi"), sem("ht_lo")
        pick_ok, rank_full, slot_ok, one_ok, gw_ok = (sem("pick_ok"), sem("rank_full"), sem("slot_ok"),
                                                      sem("one_ok"), sem("gw_ok"))
        xg_full, xg_hi, xg_lo, xg_pad = sem("xg_full"), sem("xg_hi"), sem("xg_lo"), sem("xg_pad")
        sw_full, sw_ok = sem("sw_full"), sem("sw_ok")
        gate_full, up_full, down_full = sem("gate_full"), sem("up_full"), sem("down_full")
        gate_sig, gate_free, up_free, down_free = sem("gate_sig"), sem("gate_free"), sem("up_free"), sem("down_free")
        ys_full, ys_act, ys_dve, f_full = sem("ys_full"), sem("ys_act"), sem("ys_dve"), sem("f_full")
        dve_step, act_step, pool_step = sem("dve_step"), sem("act_step"), sem("pool_step")
        pool_ready, sp_ready, pe_ready = sem("pool_ready"), sem("sp_ready"), sem("pe_ready")
        blk_step = sem("blk_step")
        y_full, y_act, y_out = sem("y_full"), sem("y_act"), sem("y_out")
        counts = {}

        def inc(ins, s):
            ins.then_inc(s, 1)
            counts[s.name] = counts.get(s.name, 0) + 1
            return ins

        PER = dict(tile_full=NTILE, tile_act=NT_ACT, tile_dve=NT_DVE, cur_ok=2, h_f=8, h_hi=8, h_lo=8,
                   pads=1, conv_b=POOL_CHUNKS, conv_dve=8 - POOL_CHUNKS, sq_qk=10, ck_full=1, ck_ok=1,
                   kn_full=1, kn_ok=1, rms_full=10, rms_std=10, qk_norm=10, rope_full=5, rope_ok=5, swap_ok=2,
                   s_full=48, s_max=48, p_exp=48, p_norm=48, pt_full=48, pt_act=24, pt_dve=24, o_full=12, o_hi=12,
                   o_lo=12, opa_hi=8, opa_lo=8, sqb=8, lnb_full=2, lnb_msq=1, lnb_var=1,
                   lnb_std=1, lnb_norm=1, lnb_aff=8, opb_f=8, opb_hi=8, opb_lo=8, m_ok=8, opm_hi=8, opm_lo=8,
                   z_ok=8, z_sq=16, ln_full=4, ln_msq=2, ln_var=2, ln_std=2, ln_norm=2, x_ok=16, h2_ok=8,
                   lg_full=1, lg_ok=1, lt_full=1, score_ok=1, ht_full=6, ht_hi=6, ht_lo=6, pick_ok=1, rank_full=1,
                   slot_ok=1, one_ok=3, gw_ok=3, xg_full=16, xg_hi=16, xg_lo=16, xg_pad=1, sw_full=6, sw_ok=6,
                   ys_full=12, ys_act=6, ys_dve=6, f_full=8, dve_step=DVE_STEPS, act_step=ACT_STEPS,
                   pool_step=POOL_STEPS)

        AHEAD = ("tile_dve", "z_ok", "x_ok", "o_full")

        def waiter(eng, layer):
            def wait(s, n):
                eng.wait_ge(s, layer * PER[s.name] + n + (s.name in AHEAD))
            return wait

        def stepper(eng, layer, s):
            k = [0]

            def step(ins):
                inc(ins, s)
                k[0] += 1
                eng.wait_ge(s, layer * PER[s.name] + k[0])
            return step

        def wait_z(wait, k, ch):
            if k == 0:
                wait(tile_dve, dve_count(MIX.index(("o", ch // 2)), ch % 2))
            else:
                wait(z_ok, ch + 1)

        def wait_conv(wait, ch):
            if ch < POOL_CHUNKS:
                wait(conv_b, ch + 1)
            else:
                wait(conv_dve, ch - POOL_CHUNKS + 1)

        def counter(eng, name):
            r = ctx.enter_context(eng.register(name))
            eng.reg_mov(r, 2)
            return r

        def load_slots(eng, ex):
            at = bass.ds(ex, 1) if not isinstance(ex, int) else slice(ex, ex + 1)
            return eng.value_load(slots_i[0:1, at], min_val=1, max_val=SLOT_STEP * 769)

        def unpack(eng, slots):
            why = "the table holds 512 * (0..768) + (1..384)"
            return (nc.s_assert_within(eng.snap(slots // SLOT_STEP), 0, 768, skip_runtime_bounds_check_because=why),
                    nc.s_assert_within(eng.snap(slots % SLOT_STEP), 1, 384, skip_runtime_bounds_check_because=why))

        def expert_panels(eng, held, panel):
            eng.reg_mov(held, load_slots(eng, 0))
            here = unpack(eng, eng.snap(held))
            for i, (kind, half) in enumerate(EXPERT_FIRST):
                panel(kind, half, NMIX + i, 0, 0, here)
            with eng.Fori(0, NEXP - 1) as ex:
                following = eng.snap(ex + 1)
                here = unpack(eng, eng.snap(held))
                eng.reg_mov(held, load_slots(eng, following))
                ahead = unpack(eng, eng.snap(held))
                for i, (kind, half) in enumerate(EXPERT_LOOP):
                    if kind == "down":
                        panel(kind, half, NMIX + 4 + i, ex, ex, here)
                    else:
                        panel(kind, half, NMIX + 4 + i, ex, following, ahead)
            here = unpack(eng, eng.snap(held))
            for i, (kind, half) in enumerate(EXPERT_LAST):
                panel(kind, half, NPANEL - 2 + i, 0, NEXP - 1, here)

        def two(eng, n, kind, width):
            return PS[:, bass.ds(eng.snap(n % 2 + BANK[kind]), 1), 0:width]

        def block_at(eng, start, rel):
            at = eng.snap(start + rel)
            return nc.s_assert_within(at, 0, 768, skip_runtime_bounds_check_because="slots end at 768")

        def wait_iota(eng, layer):
            eng.wait_ge(iota_in, layer * 16 + 16)

        block = ctx.enter_context(nc.Block())

        @block.sync
        def _(sp):
            def panel_source(layer, kind, j):
                cols = slice(j * PCOL, (j + 1) * PCOL)
                if kind == "ada":
                    w = w_ada
                elif kind in ("wa", "wb", "wc", "o"):
                    w = dict(wa=w_a_out, wb=w_b_out, wc=w_c_out, o=w_o)[kind]
                else:
                    w = w_in
                    cols = slice(COLS[kind] + j * PCOL, COLS[kind] + (j + 1) * PCOL)
                return w[bass.ds(layer, 1), :, cols].rearrange("l (k p) n -> p (l k) n", p=P)

            with sp.Fori(0, DEPTH) as layer:
                base = layer * NPANEL
                for n, (kind, j) in enumerate(MIX):
                    src = panel_source(layer, kind, j)
                    sp.wait_ge(lo_done, base + n + 1)
                    if (kind, j) == ("ab", 0):
                        sp.sem_inc(sp_ready, 1)
                    sp.dma_start(stage[:, n % STAGES, :].rearrange("p (k n) -> p k n", k=8), src
                                 ).then_inc(landed[n % STAGES], 16)

                def load(kind, half, at, loop, expert):
                    e = bass.ds(expert, 1)
                    if kind == "down":
                        src = w_down[bass.ds(layer, 1), e, :, half * 512:(half + 1) * 512]
                        k = 4
                    else:
                        c0 = half * PCOL + (512 if kind == "up" else 0)
                        src = w_gate_up[bass.ds(layer, 1), e, :, c0:c0 + PCOL]
                        k = 8
                    src = src.rearrange("l e (k p) n -> p (l e k) n", p=P)
                    sp.wait_ge(lo_done, base + 6 * loop + at + 1)
                    sp.dma_start(stage[:, at % STAGES, :].rearrange("p (k n) -> p k n", k=k), src
                                 ).then_inc(landed[at % STAGES], 16)

                for i, (kind, half) in enumerate(EXPERT_FIRST):
                    load(kind, half, NMIX + i, 0, 0)
                with sp.Fori(0, NEXP - 1) as ex:
                    for i, (kind, half) in enumerate(EXPERT_LOOP):
                        load(kind, half, NMIX + 4 + i, ex, ex if kind == "down" else sp.snap(ex + 1))
                for i, (kind, half) in enumerate(EXPERT_LAST):
                    load(kind, half, NPANEL - 2 + i, 0, NEXP - 1)

        @block.gpsimd
        def _(pool):
            with pool.Fori(0, DEPTH) as layer:
                wait = waiter(pool, layer)
                step = stepper(pool, layer, pool_step)
                for ch in range(POOL_CHUNKS):
                    wait(tile_dve, dve_count(MIX.index(("bu", ch // 2)), ch % 2))

                    def tap(out, t):
                        return pool.tensor_tensor(out, BIN[:, ch, t:t + 399],
                                                  cur[:, ch, CONVB + t:CONVB + t + 1].broadcast_to([P, 399]), ALU.mult)
                    step(tap(BACC[:, ch, :], 0))
                    for t in range(1, 31):
                        step(tap(std[:, 0:399], t))
                        step(pool.tensor_tensor(BACC[:, ch, :], BACC[:, ch, :], std[:, 0:399], ALU.add))
                    inc(pool.tensor_tensor(BACC[:, ch, :], BACC[:, ch, :],
                                           cur[:, ch, CONVBB:CONVBB + 1].broadcast_to([P, 399]), ALU.add), conv_b)
                wait_iota(pool, layer)
                wait(slot_ok, 1)
                pool.sem_inc(pool_ready, 1)
                for t in range(3):
                    pool.tensor_scalar(GW[:, t, :], iota768, pick_s[:, 0, t:t + 1], pick_w[:, 0, t:t + 1],
                                       ALU.is_equal, ALU.mult)
                    step(pool.tensor_scalar(gw_tmp[:, t, :], iota768, pick_s[:, 1, t:t + 1], pick_w[:, 1, t:t + 1],
                                            ALU.is_equal, ALU.mult))
                    inc(pool.tensor_tensor(GW[:, t, :], GW[:, t, :], gw_tmp[:, t, :], ALU.add), gw_ok)

        @block.scalar
        def _(act):
            copy, sigm, square, ident_f = ACT.Copy, ACT.Sigmoid, ACT.Square, ACT.Identity
            loads = [(tab[:], table), (XTOK[:, 0, :], x_prompt[0]),
                     (XTOK[:, 1:3, :], x_sample[0].rearrange("(t p) n -> p t n", p=P)),
                     (wr[:], w_router.rearrange("(k p) e -> p k e", p=P)),
                     (rbias[:], router_bias.rearrange("(a e) -> a e", a=1).broadcast_to([P, 16])),
                     (PROWS[2 * NPAR:2 * NPAR + 1, :], c_ctx.rearrange("(a n) -> a n", a=1)),
                     (PROWS[2 * NPAR + 1:2 * NPAR + 2, :], c)]
            for lay in range(DEPTH):
                r = lay * NPAR
                loads += [(PROWS[r:r + 31, :], conv_b_w[lay]), (PROWS[r + CONVA:r + CONVA + 3, :], conv_a_w[lay]),
                          (PROWS[r + CONVBB:r + CONVBB + 1, :], conv_b_b[lay:lay + 1]),
                          (PROWS[r + NBG:r + NBG + 1, :], norm_b_g[lay:lay + 1]),
                          (PROWS[r + NBB:r + NBB + 1, :], norm_b_b[lay:lay + 1]),
                          (PROWS[r + LNG:r + LNG + 2, :], ln_g[lay]), (PROWS[r + LNB:r + LNB + 2, :], ln_b[lay]),
                          (PROWS[r + BADA:r + BADA + 6, :], b_ada[lay].rearrange("(s n) -> s n", s=6)),
                          (PROWS[r + QG:r + QG + 1, :].rearrange("p (r d) -> p r d", d=HEAD),
                           q_norm_g[lay:lay + 1].unsqueeze(1).broadcast_to([1, 16, HEAD])),
                          (PROWS[r + KG:r + KG + 1, :].rearrange("p (r d) -> p r d", d=HEAD),
                           k_norm_g[lay:lay + 1].unsqueeze(1).broadcast_to([1, 16, HEAD]))]
            assert len(loads) == NSMALL
            for dst, src in loads:
                act.dma_start(dst, src).then_inc(small_in, 16)
            act.preload_act_table(sigm)
            for s in (gate_sig, down_free, x_ok):
                act.sem_inc(s, 1 if s is x_ok else 2)
            act.wait_ge(pro_free_dve, 2)
            act.activation(cond[:, 1, :], cond[:, 0, :], sigm).then_inc(cond_sig, 1)
            for ch in range(8):
                act.wait_ge(pro_full, 3 + ch)
                act.activation(X[:, ch, :], PS[:, 4 + (2 + ch) % 4, 0:384], copy).then_inc(pro_free_act, 1)

            n_gate, n_down = counter(act, "act_gate"), counter(act, "act_down")
            held = counter(act, "act_held")
            with act.Fori(0, DEPTH) as layer:
                wait = waiter(act, layer)
                step = stepper(act, layer, act_step)
                base = layer * NPANEL

                def hi(at, ex=0):
                    act.wait_ge(landed[at % STAGES], (layer * (NPANEL // STAGES) + ex + at // STAGES + 1) * 16)
                    if SPLITS <= at < NMIX + SPLITS:
                        old = at - SPLITS
                        wait(tile_full, TILE0[old] + TILES_OF.get(MIX[old][0], 2))
                    elif at < SPLITS:
                        act.wait_ge(panel_used, layer * EXPERT_PANELS + at + 1)
                    else:
                        act.wait_ge(panel_used, layer * EXPERT_PANELS + 6 * ex + at - NMIX + 1)
                    act.activation(split[:, at % SPLITS, 0, :], stage[:, at % STAGES, :], copy,
                                   scale=WSCALE).then_inc(hi_done, 1)

                def layer_norm(k):
                    for ch in range(8):
                        wait_z(wait, k, ch)
                        inc(act.activation(SQ[:, ch, :], X[:, ch, :], square), z_sq)
                    wait(ln_full, 2 * k + 2)
                    inc(act.activation(std[:, 0:384], PS[:, 4, 0:384], square), ln_msq)
                    wait(ln_var, k + 1)
                    inc(act.activation(std[:, 0:384], std[:, 0:384], ACT.Sqrt, bias=eps[:, 0:1]), ln_std)
                    wait(ln_norm, k + 1)
                    for ch in range(8):
                        inc(act.activation(X[:, ch, :], X[:, ch, :], ident_f, scale=cur[:, ch, LNG + k:LNG + k + 1],
                                           bias=cur[:, ch, LNB + k:LNB + k + 1]), x_ok)

                def evacuate(n, kind, j, i):
                    t = PS[:, (TILE0[n] + i) % NPROJ, 0:384]
                    ch = 2 * j + i
                    if kind in BY_ACT:
                        wait(tile_full, TILE0[n] + i + 1)
                    if kind in ("bg", "ga", "gc", "gb"):
                        q = ("bg", "ga", "gc", "gb").index(kind) * 4 + j
                        wait(tile_dve, dve_count(G_USERS[q - 1], i) if q else 0)
                        inc(act.activation(G[:, i, :], t, sigm, scale=UNSCALE), tile_act)
                    elif kind == "q":
                        inc(act.activation(SQQ[:, ch, :], t, square, scale=UNSCALE), sq_qk)
                        inc(act.activation(Q[:, ch, :], t, copy, scale=UNSCALE), tile_act)
                    elif kind == "k":
                        inc(act.activation(SQK[:, i, :], t, square, scale=UNSCALE), sq_qk)
                        act.activation(KT[:, i, 0:128], t[:, 0:128], copy, scale=UNSCALE)
                        inc(act.activation(KT[:, i, 256:512], t[:, 128:384], copy, scale=UNSCALE), tile_act)
                    elif kind == "v":
                        inc(act.activation(V[:, (0, 2, 3)[i], :], t[:, 0:256], copy, scale=UNSCALE), tile_act)
                    elif kind == "ac":
                        wait(pads, 1)
                        if j:
                            wait(tile_dve, dve_count(MIX.index(("ab", j - 1)), i))
                        act.activation(AIN[:, i, 1:129], t[:, 0:128], copy, scale=UNSCALE)
                        inc(act.activation(AIN[:, i, 130:386], t[:, 128:384], copy, scale=UNSCALE), tile_act)
                    elif kind == "ab":
                        wait(tile_dve, dve_count(n, i))
                        inc(act.activation(OPA[:, 0, ch, :], Y[:, i, :], copy), opa_hi)
                    elif kind == "wb":
                        wait(m_ok, ch + 1)
                        inc(act.activation(OPM[:, 0, ch, :], M[:, ch, :], copy, scale=UNSCALE), opm_hi)

                hi(0)
                hi(1)
                for n, (kind, j) in enumerate(MIX):
                    hi(n + 2)
                    b = n - ATT0
                    attend = 0 <= b < NBATCH
                    nk = 128 if b % 3 == 0 else 384
                    if (kind, j) == ("bg", 0):
                        for ch in range(8):
                            wait(h_f, ch + 1)
                            inc(act.activation(H[:, 0, ch, :], HF[:, ch, :], copy), h_hi)
                        act.dma_start(KC, cache_k[0, bass.ds(layer, 1)].rearrange("l s g d -> s (l g d)")
                                      ).then_inc(kv_in, 16)
                        act.dma_start(V[:, 1, :], cache_v[0, bass.ds(layer, 1)].rearrange("l s g d -> s (l g d)")
                                      ).then_inc(kv_in, 16)
                    if (kind, j) == ("ga", 0):
                        act.wait_ge(kv_out, layer * 32 + 32)
                    if attend:
                        for i in range(4):
                            wait(s_max, 4 * b + i + 1)
                            if b:
                                wait(pt_full, 4 * (b - 1) + i + 1)
                            inc(act.activation(PR[:, i, 0:nk], PS[:, 4 + i, 0:nk], ACT.Exp,
                                               bias=mx[:, 4 * b + i:4 * b + i + 1],
                                               accum_out=rsum[:, 0, 4 * b + i:4 * b + i + 1]), p_exp)
                    for i in range(TILES_OF.get(kind, 2)):
                        evacuate(n, kind, j, i)
                        if attend and i == 0:
                            for h in (0, 2):
                                wait(pt_full, 4 * b + h + 1)
                                wait(o_full, b)
                                inc(act.activation(PT[:, 0:nk // 128, h, :],
                                                   PS[:, 4 + h, 0:nk].rearrange("p (k q) -> p k q", q=128), copy),
                                    pt_act)
                    if attend:
                        wait(o_full, b + 1)
                        inc(act.activation(OPC[:, 0, 2 * (b // 3):2 * (b // 3) + 2, (b % 3) * 128:(b % 3 + 1) * 128],
                                           PS[:, 3, 0:256].rearrange("p (c q) -> p c q", c=2), copy), o_hi)
                    if (kind, j) == ("ac", 0):
                        wait(ck_full, 1)
                        inc(act.activation(KT[:, :, 128:256],
                                           PS[:, 3, 0:256].rearrange("p (c t) -> p c t", c=2), copy), ck_ok)
                        for i in range(10):
                            wait(rms_full, i + 1)
                            if i > 1:
                                wait(qk_norm, i - 1)
                            inc(act.activation(RT[:, i % 2, :], PS[:, 4 + i % 4, 0:384], ACT.Sqrt, bias=eps[:, 1:2]),
                                rms_std)
                    if (kind, j) == ("ax", 0):
                        wait(kn_full, 1)
                        inc(act.activation(KOUT, PS[:, 3, 0:256], copy), kn_ok)
                        wait(kn_ok, 1)
                        act.dma_start(new_k[0, bass.ds(layer, 1)].rearrange("l s g d -> s (l g d)"), KOUT
                                      ).then_inc(kv_out, 16)
                        wait(tile_act, act_count(MIX.index(("v", 0)), 2))
                        act.dma_start(new_v[0, bass.ds(layer, 1)].rearrange("l s g d -> s (l g d)"), V[:, 0, :]
                                      ).then_inc(kv_out, 16)
                        wait(rope_ok, 5)
                        wait(ck_ok, 1)
                        inc(act.activation(KTS[64:128], KT[0:64], copy), swap_ok)
                        inc(act.activation(KTS[0:64], KT[64:128], copy), swap_ok)
                    if n == LNB_AT:
                        for ch in range(8):
                            wait_conv(wait, ch)
                            inc(act.activation(SQB[:, ch, :], BACC[:, ch, :], square), sqb)
                        wait(lnb_full, 2)
                        inc(act.activation(std[:, 0:399], PS[:, 4, 0:399], square), lnb_msq)
                        wait(lnb_var, 1)
                        inc(act.activation(std[:, 0:399], std[:, 0:399], ACT.Sqrt, bias=eps[:, 2:3]), lnb_std)
                    if LNB_AT < n <= LNB_AT + 2:
                        wait(lnb_norm, 1)
                        for ch in range(4 * (n - LNB_AT - 1), 4 * (n - LNB_AT)):
                            gain, bias = cur[:, ch, NBG:NBG + 1], cur[:, ch, NBB:NBB + 1]
                            step(act.activation(SQB[:, ch, :], BACC[:, ch, :], sigm, scale=gain, bias=bias))
                            inc(act.activation(BACC[:, ch, :], BACC[:, ch, :], ident_f, scale=gain, bias=bias),
                                lnb_aff)
                        for ch in range(4 * (n - LNB_AT - 1), 4 * (n - LNB_AT)):
                            wait(opb_f, ch + 1)
                            act.activation(OPB[:, 0, ch, 0:128], BACC[:, ch, 0:128], copy)
                            inc(act.activation(OPB[:, 0, ch, 128:384], BACC[:, ch, 143:399], copy), opb_hi)

                layer_norm(0)
                act.dma_start(iota768, iota).then_inc(iota_in, 16)
                wait(lg_full, 1)
                inc(act.activation(LG, PS[0:16, 6, 0:384], copy), lg_ok)
                wait(lt_full, 1)
                inc(act.activation(score, PS[:, 7, 0:48].rearrange("p (t e) -> p t e", t=3), sigm), score_ok)
                for i in range(6):
                    wait(ht_full, i + 1)
                    inc(act.activation(HTOK[:, 0, i // 2, (i % 2) * 512:(i % 2 + 1) * 512], PS[:, i, :], copy), ht_hi)
                for i in range(16):
                    wait(xg_full, i + 1)
                    inc(act.activation(XG[:, 0, i // 2, (i % 2) * 384:(i % 2 + 1) * 384], PS[:, i % 4, 0:384], copy),
                        xg_hi)
                for i in range(6):
                    wait(sw_full, i + 1)
                    inc(act.activation(SW[:, i, :], PS[:, 4 + i % 4, 0:384], copy), sw_ok)

                def panel(kind, half, at, loop, expert, slots):
                    start, cnt = slots
                    if at < NPANEL - 2:
                        hi(at + 2, loop)
                    if kind == "gate":
                        with act.Fori(0, cnt, BLK):
                            n = act.snap(n_gate)
                            tile = two(act, n, kind, 2 * BLK).rearrange("p b (c s) -> p b c s", c=2)
                            sig = SIG[:, bass.ds(act.snap(n % 2), 1)]
                            before = act.snap(n - 1)
                            act.reg_add(n_gate, n_gate, 1)
                            now = act.snap(n_gate)
                            act.wait_ge(gate_free, before)
                            act.wait_ge(gate_full, now)
                            act.activation(sig, tile, sigm, scale=UNSCALE).then_inc(gate_sig, 1)
                    if kind == "down":
                        with act.Fori(0, cnt, BLK) as rel:
                            first = block_at(act, start, rel)
                            before = act.snap(n_down)
                            tile = two(act, before, kind, 4 * BLK).rearrange("p b (c s) -> p (b c) s", c=4)
                            act.reg_add(n_down, n_down, 1)
                            now = act.snap(n_down)
                            act.wait_ge(down_free, before)
                            act.wait_ge(down_full, now)
                            act.activation(YT[:, 4 * half:4 * half + 4, bass.ds(first, BLK)], tile, copy,
                                           scale=UNSCALE).then_inc(down_free, 1)

                expert_panels(act, held, panel)

                for i in range(0, 12, 2):
                    wait(ys_full, i + 1)
                    inc(act.activation(YS[:, i // 2, 0:512], PS[:, 4 + i % 4, :], copy), ys_act)
                layer_norm(1)

            for i in range(6):
                act.wait_ge(y_full, i + 1)
                act.activation(OUT[:, i // 2, (i % 2) * 512:(i % 2 + 1) * 512], PS[:, i, :], copy).then_inc(y_act, 1)
            act.wait_ge(y_act, 6)
            act.dma_start(y_prompt[0], OUT[:, 0, :]).then_inc(y_out, 16)
            act.dma_start(y_sample[0].rearrange("(t p) n -> p t n", p=P), OUT[:, 1:3, :]).then_inc(y_out, 16)
            act.wait_ge(kv_out, 32 * DEPTH)
            act.wait_ge(y_out, 32)

        @block.vector
        def _(dve):
            dve.memset(eps[:, 0:1], LN_EPS / ALPHA ** 2)
            dve.memset(eps[:, 2:3], LN_EPS)
            dve.memset(eps[:, 1:2], RMS_EPS).then_inc(eps_ok, 1)
            dve.sem_inc(lo_done, STAGES)
            for s in (gate_free, up_free, tile_dve, z_ok):
                dve.sem_inc(s, 2 if s in (gate_free, up_free) else 1)
            dve.sem_inc(blk_step, 4)
            for half in range(2):
                dve.wait_ge(pro_full, half + 1)
                src = PS[:, 4 + half, 0:4 * (DEPTH * NPAR + 2)].rearrange("p (c r) -> p c r", c=4)
                for lay in range(DEPTH):
                    dst = params[:, lay, :].rearrange("p (c r) -> p c r", c=8)[:, 4 * half:4 * half + 4, :]
                    dve.tensor_copy(dst, src[:, :, lay * NPAR:(lay + 1) * NPAR])
                dve.tensor_copy(cond[:, 0, 8 * half:8 * half + 8].rearrange("p (c g) -> p c g", c=4),
                                src[:, :, DEPTH * NPAR:DEPTH * NPAR + 2]).then_inc(pro_free_dve, 1)
            dve.wait_ge(cond_sig, 1)
            dve.tensor_tensor(cond[:, 2, :], cond[:, 0, :], cond[:, 1, :], ALU.mult).then_inc(cond_ok, 1)
            dve.wait_ge(cond_ok, 1)
            silu = cond[:, 2, :].rearrange("p (c g) -> p c g", c=8)
            dve.tensor_copy(cond_split[:, 0], silu).then_inc(cond_ok, 1)
            dve.wait_ge(cond_ok, 2)
            dve.tensor_tensor(cond_split[:, 1], silu, cond_split[:, 0], ALU.subtract).then_inc(cond_ok, 1)

            n_gate, n_up = counter(dve, "dve_gate"), counter(dve, "dve_up")
            held = counter(dve, "dve_held")
            with dve.Fori(0, DEPTH) as layer:
                wait = waiter(dve, layer)
                step = stepper(dve, layer, dve_step)
                base = layer * NPANEL

                def lo(at, ex=0):
                    dve.wait_ge(hi_done, base + 6 * ex + at + 1)
                    dve.scalar_tensor_tensor(split[:, at % SPLITS, 1, :], stage[:, at % STAGES, :], WSCALE,
                                             split[:, at % SPLITS, 0, :], op0=ALU.mult, op1=ALU.subtract
                                             ).then_inc(lo_done, 1)

                def normalise(x, mean, width):
                    s = std[:, 0:width]
                    step(dve.reciprocal(s, s))
                    step(dve.tensor_tensor(x, x, mean.unsqueeze(1).broadcast_to([P, 8, width]), ALU.subtract))
                    return dve.tensor_tensor(x, x, s.unsqueeze(1).broadcast_to([P, 8, width]), ALU.mult)

                def variance(width):
                    s = std[:, 0:width]
                    step(dve.scalar_tensor_tensor(s, s, -1.0, PS[:, 5, 0:width], op0=ALU.mult, op1=ALU.add))
                    return dve.tensor_scalar(s, s, 0.0, None, ALU.max)

                def layer_norm(k):
                    wait(ln_msq, k + 1)
                    inc(variance(384), ln_var)
                    wait(ln_std, k + 1)
                    inc(normalise(X, PS[:, 4, 0:384], 384), ln_norm)

                def evacuate(n, kind, j, i):
                    t = PS[:, (TILE0[n] + i) % NPROJ, 0:384]
                    ch = 2 * j + i
                    if kind not in BY_ACT:
                        wait(tile_full, TILE0[n] + i + 1)
                    if kind == "ada":
                        s, c0 = j // 4, 2 * (j % 4)
                        inc(dve.scalar_tensor_tensor(
                            mod[:, s, c0:c0 + 2, :], t[:, 0:4].rearrange("p (c g) -> p c g", c=2), UNSCALE,
                            cur[:, c0:c0 + 2, BADA + s:BADA + s + 1].broadcast_to([P, 2, 2]),
                            op0=ALU.mult, op1=ALU.add), tile_dve)
                        if j in (7, 11, 19, 23):
                            wait(tile_dve, dve_count(n, 0))
                        if j in (7, 19):
                            step(dve.tensor_scalar(mod[:, s], mod[:, s], 1.0, None, ALU.add))
                        if j == 11:
                            step(dve.tensor_scalar(mod[:, s], mod[:, s], UNSCALE / ALPHA, None, ALU.mult))
                        if j == 23:
                            step(dve.tensor_scalar(mod[:, s], mod[:, s], 1 / ALPHA, None, ALU.mult))
                    elif kind == "bu":
                        wait(tile_act, act_count(n - 1, i))
                        dve.scalar_tensor_tensor(BIN[:, ch, 15:143], t[:, 0:128], UNSCALE, G[:, i, 0:128],
                                                 op0=ALU.mult, op1=ALU.mult)
                        inc(dve.scalar_tensor_tensor(BIN[:, ch, 158:414], t[:, 128:384], UNSCALE, G[:, i, 128:384],
                                                     op0=ALU.mult, op1=ALU.mult), tile_dve)
                    elif kind == "ax":
                        wait(tile_act, act_count(n - 1, i))
                        dve.scalar_tensor_tensor(AIN[:, i, 1:129], t[:, 0:128], UNSCALE, AIN[:, i, 1:129],
                                                 op0=ALU.mult, op1=ALU.mult)
                        inc(dve.scalar_tensor_tensor(AIN[:, i, 130:386], t[:, 128:384], UNSCALE, AIN[:, i, 130:386],
                                                     op0=ALU.mult, op1=ALU.mult), tile_dve)
                        wait(tile_dve, dve_count(n, i))
                        step(dve.tensor_scalar(ACV[:, i, :], AIN[:, i, 0:385], cur[:, ch, CONVA:CONVA + 1], None,
                                               ALU.mult))
                        for tap in (1, 2):
                            step(dve.scalar_tensor_tensor(ACV[:, i, :], AIN[:, i, tap:tap + 385],
                                                          cur[:, ch, CONVA + tap:CONVA + tap + 1], ACV[:, i, :],
                                                          op0=ALU.mult, op1=ALU.add))
                    elif kind == "ab":
                        if j:
                            wait(opa_lo, ch - 1)
                        dve.scalar_tensor_tensor(Y[:, i, 0:128], t[:, 0:128], UNSCALE, ACV[:, i, 0:128],
                                                 op0=ALU.mult, op1=ALU.mult)
                        inc(dve.scalar_tensor_tensor(Y[:, i, 128:384], t[:, 128:384], UNSCALE, ACV[:, i, 129:385],
                                                     op0=ALU.mult, op1=ALU.mult), tile_dve)
                        wait(opa_hi, ch + 1)
                        inc(dve.tensor_tensor(OPA[:, 1, ch, :], Y[:, i, :], OPA[:, 0, ch, :], ALU.subtract), opa_lo)
                    elif kind == "wa":
                        wait(tile_act, act_count(n - 1, i))
                        inc(dve.tensor_tensor(M[:, ch, :], t, G[:, i, :], ALU.mult), tile_dve)
                    elif kind in ("wc", "wb"):
                        wait(tile_act, act_count(n - 1, i))
                        inc(dve.tensor_tensor(Y[:, i, :], t, G[:, i, :], ALU.mult), tile_dve)
                        wait(tile_dve, dve_count(n, i))
                        ins = dve.tensor_tensor(M[:, ch, :], M[:, ch, :], Y[:, i, :], ALU.add)
                        if kind == "wc":
                            step(ins)
                        else:
                            inc(ins, m_ok)
                            wait(opm_hi, ch + 1)
                            inc(dve.scalar_tensor_tensor(OPM[:, 1, ch, :], M[:, ch, :], UNSCALE, OPM[:, 0, ch, :],
                                                         op0=ALU.mult, op1=ALU.subtract), opm_lo)
                    elif kind == "o":
                        for g, cols in GRPS:
                            ins = dve.scalar_tensor_tensor(X[:, ch, cols], t[:, cols], mod[:, 2, ch, g:g + 1],
                                                           X[:, ch, cols], op0=ALU.mult, op1=ALU.add)
                        inc(ins, tile_dve)

                wait(x_ok, 0)
                inc(dve.tensor_copy(cur[:].rearrange("p c r -> p (c r)"), params[:, bass.ds(layer, 1), :].rearrange(
                    "p l n -> p (l n)")), cur_ok)
                wait(cur_ok, 1)
                inc(dve.tensor_scalar(qg8[:], cur[:, 0, QG:QG + 1], HEAD ** -0.5, None, ALU.mult), cur_ok)
                lo(0)
                lo(1)
                for n, (kind, j) in enumerate(MIX):
                    lo(n + 2)
                    b = n - ATT0
                    attend = 0 <= b < NBATCH
                    nk = 128 if b % 3 == 0 else 384
                    if attend:
                        for i in range(4):
                            wait(s_full, 4 * b + i + 1)
                            inc(dve.tensor_reduce(mx[:, 4 * b + i:4 * b + i + 1], PS[:, 4 + i, 0:nk], AX.X, ALU.max,
                                                  negate=True), s_max)
                        for i in range(4):
                            at = slice(4 * b + i, 4 * b + i + 1)
                            wait(p_exp, 4 * b + i + 1)
                            step(dve.reciprocal(rsum[:, 1, at], rsum[:, 0, at]))
                            inc(dve.tensor_scalar(PR[:, i, 0:nk], PR[:, i, 0:nk], rsum[:, 1, at], None, ALU.mult),
                                p_norm)
                    for i in range(TILES_OF.get(kind, 2)):
                        evacuate(n, kind, j, i)
                        if attend and i == 0:
                            for h in (1, 3):
                                wait(pt_full, 4 * b + h + 1)
                                wait(o_full, b)
                                inc(dve.tensor_copy(PT[:, 0:nk // 128, h, :],
                                                    PS[:, 4 + h, 0:nk].rearrange("p (k q) -> p k q", q=128)), pt_dve)
                    if attend:
                        wait(o_hi, b + 1)
                        at = (slice(2 * (b // 3), 2 * (b // 3) + 2), slice((b % 3) * 128, (b % 3 + 1) * 128))
                        inc(dve.tensor_tensor(OPC[:, 1, at[0], at[1]], PS[:, 3, 0:256].rearrange("p (c q) -> p c q", c=2),
                                              OPC[:, 0, at[0], at[1]], ALU.subtract), o_lo)
                    for ch, tap in CONV_TAPS.get(n, ()):
                        if tap == 0:
                            wait(tile_dve, dve_count(MIX.index(("bu", ch // 2)), ch % 2))
                            step(dve.tensor_scalar(BACC[:, ch, :], BIN[:, ch, 0:399], cur[:, ch, CONVB:CONVB + 1],
                                                   cur[:, ch, CONVBB:CONVBB + 1], ALU.mult, ALU.add))
                            continue
                        ins = dve.scalar_tensor_tensor(BACC[:, ch, :], BIN[:, ch, tap:tap + 399],
                                                       cur[:, ch, CONVB + tap:CONVB + tap + 1], BACC[:, ch, :],
                                                       op0=ALU.mult, op1=ALU.add)
                        if tap < 30:
                            step(ins)
                        else:
                            inc(ins, conv_dve)
                    if (kind, j) == ("ada", 7):
                        for at in (slice(0, 15), slice(143, 158), slice(414, 429)):
                            dve.memset(BIN[:, :, at], 0.0)
                        for at in (slice(0, 1), slice(129, 130), slice(386, 387)):
                            ins = dve.memset(AIN[:, :, at], 0.0)
                        inc(ins, pads)
                        wait(pads, 1)
                        for ch in range(8):
                            for g, cols in GRPS:
                                ins = dve.tensor_scalar(HF[:, ch, cols], X[:, ch, cols], mod[:, 1, ch, g:g + 1],
                                                        mod[:, 0, ch, g:g + 1], ALU.mult, ALU.add)
                            inc(ins, h_f)
                        for ch in range(8):
                            wait(h_hi, ch + 1)
                            inc(dve.tensor_tensor(H[:, 1, ch, :], HF[:, ch, :], H[:, 0, ch, :], ALU.subtract), h_lo)
                    if (kind, j) == ("ac", 0):
                        for i in range(10):
                            r = RT[:, i % 2, :]
                            wait(rms_std, i + 1)
                            step(dve.reciprocal(r, r))
                            if i < 8:
                                inc(dve.scalar_tensor_tensor(Q[:, i, :], Q[:, i, :], qg8[:, 0:1], r, op0=ALU.mult,
                                                             op1=ALU.mult), qk_norm)
                            else:
                                for k_at, r_at in ((slice(0, 128), slice(0, 128)), (slice(256, 512), slice(128, 384))):
                                    ins = dve.scalar_tensor_tensor(KT[:, i - 8, k_at], KT[:, i - 8, k_at],
                                                                   cur[:, 0, KG:KG + 1], r[:, r_at], op0=ALU.mult,
                                                                   op1=ALU.mult)
                                inc(ins, qk_norm)
                    if (kind, j) == ("ax", 0):
                        cos2 = cos_t.unsqueeze(1).broadcast_to([P, 2, 256])
                        sin2 = sin_t.unsqueeze(1).broadcast_to([P, 2, 256])
                        for pr in range(5):
                            v = Q[:, 2 * pr:2 * pr + 2, 128:384] if pr < 4 else KT[:, :, 256:512]
                            wait(rope_full, pr + 1)
                            step(dve.tensor_tensor(ROT, PS[:, 4 + pr % 4, :].rearrange("p (c t) -> p c t", c=2), sin2,
                                                   ALU.mult))
                            step(dve.tensor_tensor(v, v, cos2, ALU.mult))
                            inc(dve.tensor_tensor(v, v, ROT, ALU.add), rope_ok)
                            wait(rope_ok, pr + 1)
                    if n == LNB_AT:
                        wait(lnb_msq, 1)
                        inc(variance(399), lnb_var)
                        wait(lnb_std, 1)
                        inc(normalise(BACC, PS[:, 4, 0:399], 399), lnb_norm)
                    if LNB_AT < n <= LNB_AT + 2:
                        for ch in range(4 * (n - LNB_AT - 1), 4 * (n - LNB_AT)):
                            wait(lnb_aff, ch + 1)
                            inc(dve.tensor_tensor(BACC[:, ch, :], BACC[:, ch, :], SQB[:, ch, :], ALU.mult), opb_f)
                        for ch in range(4 * (n - LNB_AT - 1), 4 * (n - LNB_AT)):
                            wait(opb_hi, ch + 1)
                            dve.tensor_tensor(OPB[:, 1, ch, 0:128], BACC[:, ch, 0:128], OPB[:, 0, ch, 0:128],
                                              ALU.subtract)
                            inc(dve.tensor_tensor(OPB[:, 1, ch, 128:384], BACC[:, ch, 143:399], OPB[:, 0, ch, 128:384],
                                                  ALU.subtract), opb_lo)

                layer_norm(0)
                for ch in range(8):
                    wait(x_ok, ch + 1)
                    for g, cols in GRPS:
                        ins = dve.tensor_scalar(H2[:, ch, cols], X[:, ch, cols], mod[:, 4, ch, g:g + 1],
                                                mod[:, 3, ch, g:g + 1], ALU.mult, ALU.add)
                    inc(ins, h2_ok)

                def first_of_max(x, out, n):
                    k = key[:, :, 0:n]
                    step(dve.tensor_reduce(top, x, AX.X, ALU.max))
                    step(dve.tensor_tensor(k, x, top.unsqueeze(2).broadcast_to([P, 3, n]), ALU.is_equal))
                    step(dve.scalar_tensor_tensor(k, k, -32.0, iota16[:, 0:n].unsqueeze(1).broadcast_to([P, 3, n]),
                                                  op0=ALU.mult, op1=ALU.add))
                    step(dve.tensor_reduce(top, k, AX.X, ALU.min))
                    step(dve.tensor_tensor(out, k, top.unsqueeze(2).broadcast_to([P, 3, n]), ALU.is_equal))

                wait(score_ok, 1)
                step(dve.tensor_tensor(sel, score, rbias[:].unsqueeze(1).broadcast_to([P, 3, 16]), ALU.add))
                four = sel.rearrange("p t (g e) -> p t g e", g=4)
                for h in range(2):
                    step(dve.tensor_tensor(pair_hi[:, h], four[:, :, :, 2 * h], four[:, :, :, 2 * h + 1], ALU.max))
                    step(dve.tensor_tensor(pair_lo[:, h], four[:, :, :, 2 * h], four[:, :, :, 2 * h + 1], ALU.min))
                step(dve.tensor_tensor(grp[:, 0], pair_hi[:, 0], pair_hi[:, 1], ALU.max))
                step(dve.tensor_tensor(grp[:, 1], pair_hi[:, 0], pair_hi[:, 1], ALU.min))
                step(dve.tensor_tensor(grp[:, 2], pair_lo[:, 0], pair_lo[:, 1], ALU.max))
                step(dve.tensor_tensor(grp[:, 1], grp[:, 1], grp[:, 2], ALU.max))
                step(dve.tensor_tensor(grp[:, 0], grp[:, 0], grp[:, 1], ALU.add))
                first_of_max(grp[:, 0], grp[:, 3], 4)
                step(dve.tensor_scalar(grp[:, 3], grp[:, 3], 1e30, -1e30, ALU.mult, ALU.add))
                step(dve.tensor_tensor(selm.rearrange("p t (g e) -> p t g e", g=4), four,
                                       grp[:, 3].unsqueeze(3).broadcast_to([P, 3, 4, 4]), ALU.add))
                first_of_max(selm, one1, 16)
                step(dve.scalar_tensor_tensor(selm, one1, -3e30, selm, op0=ALU.mult, op1=ALU.add))
                first_of_max(selm, one2, 16)
                inc(dve.tensor_tensor(picked, one1, one2, ALU.add), pick_ok)
                for h, one in enumerate((one1, one2)):
                    step(dve.tensor_tensor(sel, one, score, ALU.mult))
                    step(dve.tensor_reduce(pick_w[:, h], sel, AX.X, ALU.add))
                step(dve.tensor_tensor(top, pick_w[:, 0], pick_w[:, 1], ALU.add))
                step(dve.reciprocal(top, top))
                for h in range(2):
                    step(dve.tensor_tensor(pick_w[:, h], pick_w[:, h], top, ALU.mult))
                for i in range(6):
                    wait(ht_hi, i + 1)
                    at = slice((i % 2) * 512, (i % 2 + 1) * 512)
                    inc(dve.tensor_tensor(HTOK[:, 1, i // 2, at], PS[:, i, :], HTOK[:, 0, i // 2, at], ALU.subtract),
                        ht_lo)
                wait(rank_full, 1)
                step(dve.tensor_scalar(scan[:, 0], PS[:, 6, 48:64], 1024.0, None, ALU.mult))
                step(dve.tensor_copy(scan[:, 1], scan[:, 0]))
                a = 1
                for s in (1, 2, 4, 8):
                    dve.tensor_copy(scan[:, 3 - a, 0:s], scan[:, a, 0:s])
                    step(dve.tensor_tensor(scan[:, 3 - a, s:16], scan[:, a, s:16], scan[:, a, 0:16 - s], ALU.add))
                    a = 3 - a
                step(dve.tensor_tensor(scan[:, 3], scan[:, a], scan[:, 0], ALU.subtract))
                step(dve.scalar_tensor_tensor(slot, PS[:, 6, 0:48].rearrange("p (t e) -> p t e", t=3), 1024.0,
                                              scan[:, 3].unsqueeze(1).broadcast_to([P, 3, 16]), op0=ALU.mult,
                                              op1=ALU.add))
                for h, one in enumerate((one1, one2)):
                    step(dve.tensor_tensor(sel, one, slot, ALU.mult))
                    step(dve.tensor_reduce(pick_s[:, h], sel, AX.X, ALU.add))
                step(dve.tensor_scalar(scan[0:1, 0], scan[0:1, 0], 1.0, None, ALU.max))
                inc(dve.scalar_tensor_tensor(slots_i[0:1, :], scan[0:1, 3], float(SLOT_STEP), scan[0:1, 0],
                                             op0=ALU.mult, op1=ALU.add), slot_ok)
                wait_iota(dve, layer)
                for t in range(3):
                    step(dve.tensor_scalar(ONE[:, t, :], iota768, pick_s[:, 0, t:t + 1], None, ALU.is_equal))
                    inc(dve.scalar_tensor_tensor(ONE[:, t, :], iota768, pick_s[:, 1, t:t + 1], ONE[:, t, :],
                                                 op0=ALU.is_equal, op1=ALU.add), one_ok)
                inc(dve.memset(XG[:, :, :, 768:896], 0.0), xg_pad)
                for i in range(16):
                    at = slice((i % 2) * 384, (i % 2 + 1) * 384)
                    wait(xg_hi, i + 1)
                    inc(dve.tensor_tensor(XG[:, 1, i // 2, at], PS[:, i % 4, 0:384], XG[:, 0, i // 2, at],
                                          ALU.subtract), xg_lo)

                def panel(kind, half, at, loop, expert, slots):
                    cnt = slots[1]
                    if at < NPANEL - 2:
                        lo(at + 2, loop)
                    if kind == "gate":
                        with dve.Fori(0, cnt, BLK) as rel:
                            n = dve.snap(n_gate)
                            tile = two(dve, n, kind, 2 * BLK).rearrange("p b (c s) -> p (b c) s", c=2)
                            sig = SIG[:, bass.ds(dve.snap(n % 2), 1)].rearrange("p b c s -> p (b c) s")
                            dve.reg_add(n_gate, n_gate, 1)
                            now = dve.snap(n_gate)
                            dve.wait_ge(gate_sig, now)
                            dve.scalar_tensor_tensor(GT[:, :, bass.ds(rel, BLK)], tile, UNSCALE, sig, op0=ALU.mult,
                                                     op1=ALU.mult).then_inc(gate_free, 1)
                    if kind == "up":
                        with dve.Fori(0, cnt, BLK) as rel:
                            silus, before = dve.snap(n_gate), dve.snap(n_up)
                            tile = two(dve, before, kind, 2 * BLK).rearrange("p b (c s) -> p (b c) s", c=2)
                            done = dve.snap(n_up) * 2
                            dve.reg_add(n_up, n_up, 1)
                            now = dve.snap(n_up)
                            dve.wait_ge(gate_free, silus)
                            dve.wait_ge(up_free, before)
                            dve.wait_ge(up_full, now)
                            hid = [HID[:, s, 2 * half:2 * half + 2, bass.ds(rel, BLK)] for s in range(2)]
                            dve.scalar_tensor_tensor(HF2, tile, UNSCALE, GT[:, :, bass.ds(rel, BLK)], op0=ALU.mult,
                                                     op1=ALU.mult).then_inc(blk_step, 1)
                            dve.wait_ge(blk_step, done + 1)
                            dve.tensor_copy(hid[0], HF2).then_inc(blk_step, 1)
                            dve.wait_ge(blk_step, done + 2)
                            dve.tensor_tensor(hid[1], HF2, hid[0], ALU.subtract).then_inc(up_free, 1)

                expert_panels(dve, held, panel)

                for i in range(1, 12, 2):
                    wait(ys_full, i + 1)
                    inc(dve.tensor_copy(YS[:, i // 2, 512:1024], PS[:, 4 + i % 4, :]), ys_dve)
                for ch in range(8):
                    wait(f_full, ch + 1)
                    for g, cols in GRPS:
                        ins = dve.scalar_tensor_tensor(X[:, ch, cols], PS[:, ch % 4, cols], mod[:, 5, ch, g:g + 1],
                                                       X[:, ch, cols], op0=ALU.mult, op1=ALU.add)
                    inc(ins, z_ok)
                layer_norm(1)

        @block.tensor
        def _(pe):
            pe.sem_inc(panel_used, SPLITS)
            for s in (gate_full, up_full, down_full):
                pe.sem_inc(s, 2)
            pe.sem_inc(o_full, 1)
            pe.wait_ge(small_in, 16 * NSMALL)
            rows = DEPTH * NPAR + 2
            for ch in range(8):
                ins = pe.transpose(PS[:, 4 + ch // 4, (ch % 4) * rows:(ch % 4 + 1) * rows],
                                   PROWS[0:rows, ch * P:(ch + 1) * P], ident[0:rows, 0:rows])
                if ch % 4 == 3:
                    ins.then_inc(pro_full, 1)
            for ch in range(8):
                q = 2 + ch
                if q in (4, 5):
                    pe.wait_ge(pro_free_dve, q - 3)
                if q > 5:
                    pe.wait_ge(pro_free_act, q - 5)
                for t in range(3):
                    ins = pe.transpose(PS[:, 4 + q % 4, t * P:(t + 1) * P], XTOK[:, t, ch * P:(ch + 1) * P], ident)
                ins.then_inc(pro_full, 1)
            pe.wait_ge(cond_ok, 3)

            n_gate, n_up, n_down, held = (counter(pe, f"pe_{x}") for x in ("gate", "up", "down", "held"))
            with pe.Fori(0, DEPTH) as layer:
                wait = waiter(pe, layer)
                base = layer * NPANEL

                def products(out, pairs):
                    for x, (lhsT, rhs) in enumerate(pairs):
                        ins = pe.matmul(out, lhsT, rhs, start=(x == 0), stop=(x == len(pairs) - 1))
                    return ins

                def weights(at, k):
                    return [split[:, at % SPLITS, s, :].rearrange("p (k n) -> p k n", k=k) for s in range(2)]

                def three(w, x, chunks, cols):
                    out = []
                    for k in range(chunks):
                        out += [(w[0][:, k, cols], x(0, k)), (w[0][:, k, cols], x(1, k)), (w[1][:, k, cols], x(0, k))]
                    return out

                operand = dict(wa=OPA, wb=OPB, wc=OPC, o=OPM)
                operand_ready = dict(wa=(opa_lo, 8), wb=(opb_lo, 8), wc=(o_lo, 12), o=(opm_lo, 8))

                def project(n, kind, j, i):
                    q = TILE0[n] + i
                    if q >= NPROJ:
                        act = TILE_KIND[q - NPROJ] in BY_ACT
                        wait(tile_act if act else tile_dve, tiles_freed(q - NPROJ + 1, act))
                    else:
                        wait(z_ok, 0)
                    bank = PS[:, q % NPROJ, :]
                    w = weights(n, 8)
                    x = operand.get(kind, H)
                    if kind == "ada":
                        for cc in range(2):
                            ins = products(bank[:, 2 * cc:2 * cc + 2],
                                           three(w, lambda s, k: cond_split[:, s, k, :], 8, slice(cc * P, (cc + 1) * P)))
                    elif kind == "v":
                        tok = slice(i * P, (i + 1) * P)
                        pairs = []
                        for k in range(8):
                            pairs += [(H[:, 0, k, tok], w[0][:, k, :]), (H[:, 0, k, tok], w[1][:, k, :]),
                                      (H[:, 1, k, tok], w[0][:, k, :])]
                        ins = products(bank[:, 0:256], pairs)
                    else:
                        if i == 0 and j == 0 and kind in operand_ready:
                            wait(*operand_ready[kind])
                        pairs = three(w, lambda s, k: x[:, s, k, :], 8, slice(i * P, (i + 1) * P))
                        if (kind, j, i) == ("bg", 0, 0):
                            for m, (lhsT, rhs) in enumerate(pairs):
                                if m % 3 == 0:
                                    wait(h_lo, m // 3 + 1)
                                ins = pe.matmul(bank[:, 0:384], lhsT, rhs, start=(m == 0), stop=(m == len(pairs) - 1))
                        else:
                            ins = products(bank[:, 0:384], pairs)
                    return ins

                def row_stats(k, source, squares, ready, sq_ready, full, width):
                    for ch in range(8):
                        ready(ch)
                        ins = pe.matmul(PS[:, 4, 0:width], mean_mat, source[:, ch, :], start=(ch == 0), stop=(ch == 7))
                    inc(ins, full)
                    for ch in range(8):
                        sq_ready(ch)
                        ins = pe.matmul(PS[:, 5, 0:width], mean_mat, squares[:, ch, :], start=(ch == 0), stop=(ch == 7))
                    inc(ins, full)

                def layer_norm(k):
                    row_stats(k, X, SQ, lambda ch: wait_z(wait, k, ch), lambda ch: wait(z_sq, 8 * k + ch + 1),
                              ln_full, 384)

                for n, (kind, j) in enumerate(MIX):
                    b = n - ATT0
                    attend = 0 <= b < NBATCH
                    g, t = b // 3, b % 3
                    nk = 128 if t == 0 else 384
                    keys = slice(0, 128) if t == 0 else slice(128, 512)
                    if attend:
                        for i in range(4):
                            if b == 0:
                                wait(rope_ok, 5)
                                wait(swap_ok, 2)
                            else:
                                wait((pt_act, pt_dve)[i % 2], 2 * (b - 1) + i // 2 + 1)
                            rows_of = slice(64 * (i % 2), 64 * (i % 2) + 64)
                            kt = KT if g % 2 == i % 2 else KTS
                            inc(pe.matmul(PS[:, 4 + i, 0:nk], Q[rows_of, 2 * g + i // 2, t * P:(t + 1) * P],
                                          kt[rows_of, g // 2, keys], start=True, stop=True), s_full)
                    if n == LNB_AT:
                        row_stats(0, BACC, SQB, lambda ch: wait_conv(wait, ch), lambda ch: wait(sqb, ch + 1),
                                  lnb_full, 399)
                    pe.wait_ge(lo_done, STAGES + base + n + 1)
                    tiles = TILES_OF.get(kind, 2)
                    for i in range(tiles):
                        ins = project(n, kind, j, i)
                        inc(ins, tile_full)
                        if attend and i == 0:
                            for h in range(4):
                                wait(p_norm, 4 * b + h + 1)
                                for kt in range(nk // P):
                                    ins = pe.transpose(PS[:, 4 + h, kt * P:(kt + 1) * P], PR[:, h, kt * P:(kt + 1) * P],
                                                       ident)
                                inc(ins, pt_full)
                    if attend:
                        wait(pt_act, 2 * b + 2)
                        wait(pt_dve, 2 * b + 2)
                        if b == 0:
                            wait(kn_ok, 1)
                        else:
                            wait(o_lo, b)
                        for half in range(2):
                            for kt in range(nk // P):
                                ins = pe.matmul(PS[64 * half:64 * half + 64, 3, 0:256],
                                                V[:, 0 if t == 0 else 1 + kt, 64 * g:64 * g + 64],
                                                PT[:, kt, half::2, :], start=(kt == 0), stop=(kt == nk // P - 1))
                        inc(ins, o_full)
                    if (kind, j) == ("ac", 0):
                        pe.wait_ge(kv_in, layer * 32 + 32)
                        for ch in range(2):
                            ins = pe.transpose(PS[:, 3, ch * P:(ch + 1) * P], KC[:, ch * P:(ch + 1) * P], ident)
                        inc(ins, ck_full)
                        for i in range(10):
                            wait(sq_qk, i + 1)
                            if i >= 4:
                                wait(rms_std, i - 3)
                            inc(pe.matmul(PS[:, 4 + i % 4, 0:384], head_mat, SQQ[:, i, :] if i < 8 else SQK[:, i - 8, :],
                                          start=True, stop=True), rms_full)
                    if (kind, j) == ("ax", 0):
                        wait(qk_norm, 10)
                        wait(ck_ok, 1)
                        for ch in range(2):
                            ins = pe.transpose(PS[:, 3, ch * P:(ch + 1) * P], KT[:, ch, 0:P], ident)
                        inc(ins, kn_full)
                        for pr in range(5):
                            if pr == 4:
                                wait(rope_ok, 1)
                            for x in range(2):
                                v = Q[:, 2 * pr + x, 128:384] if pr < 4 else KT[:, x, 256:512]
                                ins = pe.matmul(PS[:, 4 + pr % 4, x * 256:(x + 1) * 256], rot_mat, v, start=True,
                                                stop=True)
                            inc(ins, rope_full)

                layer_norm(0)
                for k in range(8):
                    wait(h2_ok, k + 1)
                    ins = pe.matmul(PS[0:16, 6, 0:384], wr[:, k, :], H2[:, k, :], start=(k == 0), stop=(k == 7))
                inc(ins, lg_full)
                wait(lg_ok, 1)
                for t in range(3):
                    ins = pe.matmul(PS[:, 7, 16 * t:16 * t + 16], LG[:, t * P:(t + 1) * P], ident[0:16, 0:16],
                                    start=True, stop=True)
                inc(ins, lt_full)
                for i in range(6):
                    for cc in range(4):
                        ins = pe.transpose(PS[:, i, cc * P:(cc + 1) * P],
                                           H2[:, 4 * (i % 2) + cc, (i // 2) * P:(i // 2 + 1) * P], ident)
                    inc(ins, ht_full)
                wait(pick_ok, 1)
                for t in range(3):
                    pairs = [(earlier_mat, picked[:, t, :])] + [(mean_mat, picked[:, u, :]) for u in range(t)]
                    products(PS[:, 6, 16 * t:16 * t + 16], pairs)
                inc(products(PS[:, 6, 48:64], [(mean_mat, picked[:, t, :]) for t in range(3)]), rank_full)
                wait(one_ok, 3)
                wait(ht_lo, 6)
                for i in range(16):
                    if i >= 4:
                        wait(xg_lo, i - 3)
                    ch, at = i // 2, slice((i % 2) * 384, (i % 2 + 1) * 384)
                    inc(products(PS[:, i % 4, 0:384], [(HTOK[:, s, t, ch * P:(ch + 1) * P], ONE[:, t, at])
                                                       for t in range(3) for s in range(2)]), xg_full)
                wait(xg_lo, 16)
                wait(xg_pad, 1)
                for i in range(6):
                    if i == 0:
                        wait(gw_ok, 3)
                    if i >= 4:
                        wait(sw_ok, i - 3)
                    for t in range(3):
                        ins = pe.transpose(PS[:, 4 + i % 4, t * P:(t + 1) * P], GW[:, t, i * P:(i + 1) * P], ident)
                    inc(ins, sw_full)

                wait(sw_ok, 6)
                pe.sem_inc(pe_ready, 1)

                def panel(kind, half, at, loop, expert, slots):
                    start, cnt = slots
                    w = weights(at, 4 if kind == "down" else 8)
                    with pe.Fori(0, cnt, BLK) as rel:
                        r = dict(gate=n_gate, up=n_up, down=n_down)[kind]
                        n, hidden = pe.snap(r), pe.snap(n_up)
                        tile = PS[:, bass.ds(pe.snap(n % 2 + BANK[kind]), 1), :].rearrange("p b n -> p (b n)")
                        before = pe.snap(n - 1)
                        pe.wait_ge(lo_done, STAGES + base + 6 * loop + at + 1)
                        pe.wait_ge(dict(gate=gate_free, up=up_free, down=down_free)[kind], before)
                        if kind == "down":
                            pe.wait_ge(up_free, hidden)
                            for cc in range(4):
                                ins = products(tile[:, cc * BLK:(cc + 1) * BLK],
                                               three(w, lambda s, k: HID[:, s, k, bass.ds(rel, BLK)], 4,
                                                     slice(cc * P, (cc + 1) * P)))
                            ins.then_inc(down_full, 1)
                        else:
                            first = block_at(pe, start, rel)
                            for cc in range(2):
                                ins = products(tile[:, cc * BLK:(cc + 1) * BLK],
                                               three(w, lambda s, k: XG[:, s, k, bass.ds(first, BLK)], 8,
                                                     slice(cc * P, (cc + 1) * P)))
                            ins.then_inc(gate_full if kind == "gate" else up_full, 1)
                        pe.reg_add(r, r, 1)
                    pe.matmul(PS[:, 3, 0:4], w[0][:, 0, 0:P], XG[:, 0, 0, 0:4], start=True, stop=True
                              ).then_inc(panel_used, 1)

                expert_panels(pe, held, panel)

                pe.wait_ge(down_free, pe.snap(n_down))
                for i in range(12):
                    if i >= 4:
                        wait((ys_act, ys_dve)[i % 2], (i - 4) // 2 + 1)
                    for cc in range(4):
                        ins = pe.transpose(PS[:, 4 + i % 4, cc * P:(cc + 1) * P],
                                           YT[:, 4 * (i % 2) + cc, (i // 2) * P:(i // 2 + 1) * P], ident)
                    inc(ins, ys_full)
                wait(ys_act, 6)
                wait(ys_dve, 6)
                for ch in range(8):
                    if ch >= 4:
                        wait(z_ok, ch - 3)
                    inc(products(PS[:, ch % 4, 0:384], [(YS[:, s, ch * P:(ch + 1) * P], SW[:, s, :])
                                                        for s in range(6)]), f_full)
                layer_norm(1)

            pe.wait_ge(x_ok, 16 * DEPTH + 1)
            for i in range(6):
                for cc in range(4):
                    ins = pe.transpose(PS[:, i, cc * P:(cc + 1) * P],
                                       X[:, 4 * (i % 2) + cc, (i // 2) * P:(i // 2 + 1) * P], ident)
                ins.then_inc(y_full, 1)

        off = {k: (v, counts.get(k, 0)) for k, v in PER.items() if counts.get(k, 0) != v}
        assert not off, f"signals per layer (stated, emitted): {off}"


_INS = ["x_prompt", "x_sample", "c", "c_ctx", "cache_k", "cache_v", "w_in", "conv_a_w", "w_a_out", "conv_b_w",
        "conv_b_b", "norm_b_g", "norm_b_b", "w_b_out", "q_norm_g", "k_norm_g", "w_c_out", "w_o", "w_ada", "b_ada",
        "ln_g", "ln_b", "w_router", "router_bias", "w_gate_up", "w_down"]


def kernel(**inputs):
    import concourse.bacc as bacc
    from concourse.bass_utils import run_bass_kernel_spmd

    nc = bacc.Bacc("TRN2", target_bir_lowering=False, num_devices=1)
    table, iota = shape_constants()
    arrays, args = {}, {}
    for name in _INS + ["table", "iota"]:
        a = np.ascontiguousarray(inputs[name]) if name in inputs else dict(table=table, iota=iota)[name]
        arrays[f"in_{name}"] = a
        args[name] = nc.dram_tensor(f"in_{name}", a.shape, mybir.dt.from_np(a.dtype), kind="ExternalInput").ap()
    depth = arrays["in_w_in"].shape[0]
    outs = [("y_prompt", arrays["in_x_prompt"].shape), ("y_sample", arrays["in_x_sample"].shape),
            ("new_k", (1, depth, 128, 4, 64)), ("new_v", (1, depth, 128, 4, 64))]
    for name, shape in outs:
        args[name] = nc.dram_tensor(name, shape, F32, kind="ExternalOutput").ap()
    build(nc, **args)
    r = run_bass_kernel_spmd(nc, [arrays], core_ids=[0])
    return tuple(r.results[0][name] for name, _ in outs)
```

```python
import math
from contextlib import ExitStack

import numpy as np

import concourse.bass as bass
from concourse import mybir

F32 = mybir.dt.float32
F16 = mybir.dt.float16
I32 = mybir.dt.int32
ALU = mybir.AluOpType
ACT = mybir.ActivationFunctionType
AX = mybir.AxisListType

P = 128
BLK = 128
STAGES, SPLITS = 6, 3
PCOL = 256
WSCALE = 64.0
UNSCALE = 1.0 / WSCALE
HEAD = 64
GRID_W = 64
LN_EPS, RMS_EPS = 1e-5, 1e-6

CONVB, CONVA, CONVBB, NBG, NBB, LNG, LNB, BADA, QG, KG, NPAR = 0, 31, 34, 35, 36, 37, 39, 41, 47, 48, 49


def shape_constants():
    ident = np.eye(P, dtype=np.float32)
    mean_of_model = np.full((P, P), 1.0 / 1024, np.float32)
    head_mean = np.kron(np.eye(2), np.full((HEAD, HEAD), 1.0 / HEAD)).astype(np.float32)
    rot = np.zeros((P, P), np.float32)
    for d in range(P):
        if d % 32 < 16:
            rot[d, d + 16] = -1.0
        else:
            rot[d, d - 16] = 1.0
    half = 16
    freqs = np.power(np.float32(10000.0), -np.arange(half, dtype=np.float32) / np.float32(half)).astype(np.float32)
    token = np.arange(256)
    row, col = (token // GRID_W).astype(np.float32), (token % GRID_W).astype(np.float32)
    ang = np.zeros((P, 256), np.float32)
    for d in range(P):
        pos = row if d % 64 < 32 else col
        ang[d] = pos * freqs[d % 16]
    earlier = np.triu(np.ones((P, P), np.float32), 1) / 1024
    iota16 = np.tile(np.arange(16, dtype=np.float32), (P, 1))
    table = np.concatenate(
        [ident, mean_of_model, head_mean, rot.T, earlier, np.cos(ang), np.sin(ang), iota16], axis=1)
    return np.ascontiguousarray(table, np.float32), np.tile(np.arange(768), (P, 1)).astype(np.float16)


def section_panels():
    order = [("ada", j) for j in range(8)]
    order += [("bg", 0), ("bu", 0), ("bg", 1), ("bu", 1)]
    order += [("q", j) for j in range(4)] + [("k", 0), ("v", 0)]
    order += [("bg", 2), ("bu", 2), ("bg", 3), ("bu", 3)]
    for j in range(4):
        order += [("ac", j), ("ax", j), ("ab", j)]
    for j in range(4):
        order += [("ga", j), ("wa", j)]
    ada = iter(range(8, 24))
    for s in "cb":
        for j in range(4):
            order += [("g" + s, j), ("ada", next(ada)), ("w" + s, j), ("ada", next(ada))]
    order += [("o", j) for j in range(4)]
    return order


MIX = section_panels()
NMIX = len(MIX)
NEXP = 16
SLOT_STEP = 512
EXPERT_FIRST = (("gate", 0), ("up", 0), ("gate", 1), ("up", 1))
EXPERT_LOOP = (("gate", 0), ("down", 0), ("down", 1), ("up", 0), ("gate", 1), ("up", 1))
EXPERT_LAST = (("down", 0), ("down", 1))
EXPERT_PANELS = NEXP * 6
BANK = dict(gate=0, up=4, down=6)
NPANEL = NMIX + EXPERT_PANELS
COLS = dict(ab=0, ac=1024, ax=2048, bu=3072, bg=4096, q=5120, k=6144, v=6400, ga=6656, gb=7680, gc=8704)
TILES_OF = dict(ada=1, v=3)
RMS_AT = {MIX.index(k): range(2 * i, 2 * i + 2)
          for i, k in enumerate([("q", 1), ("q", 2), ("q", 3), ("k", 0), ("v", 0)])}
ROPE_AT = {MIX.index(("bu", 2)): range(0, 4), MIX.index(("bg", 3)): range(4, 5)}
ATT0 = MIX.index(("bu", 3))
NBATCH = 12
TILE0 = []
for _kind, _j in MIX:
    TILE0.append(TILE0[-1] + _n if TILE0 else 0)
    _n = TILES_OF.get(_kind, 2)
NTILE = TILE0[-1] + _n
BY_ACT = {"bg", "q", "k", "v", "ac", "ga", "gb", "gc"}
TILE_KIND = [k for k, _j in MIX for _ in range(TILES_OF.get(k, 2))]
NPROJ = 3
GRPS = ((0, slice(0, 128)), (1, slice(128, 384)))


def tiles_freed(upto, act):
    return sum((k in BY_ACT) == act for k in TILE_KIND[:upto])


def act_count(n, i):
    return tiles_freed(TILE0[n] + i + 1, True)


def dve_count(n, i):
    return tiles_freed(TILE0[n] + i + 1, False)


NT_ACT, NT_DVE = tiles_freed(NTILE, True), tiles_freed(NTILE, False)
DVE_STEPS, ACT_STEPS, POOL_STEPS = 228, 8, 366
G_USERS = [MIX.index((k, j)) for k in ("bu", "wa", "wc", "wb") for j in range(4)]
POOL_CHUNKS = 6
_beside = [(MIX.index(("ga", 0)) + i, 5) for i in range(13)]
_taps = [(ch, t) for ch in range(POOL_CHUNKS, 8) for t in range(31)]
CONV_TAPS = {}
for _n, _k in _beside:
    CONV_TAPS[_n], _taps = _taps[:_k], _taps[_k:]
assert not _taps
SILU_AT = {MIX.index(("wc", 3)): range(0, 4), MIX.index(("gb", 0)): range(4, 8)}
LNB_AT = MIX.index(("wc", 1))


def build(nc, x_prompt, x_sample, c, c_ctx, cache_k, cache_v, w_in, conv_a_w, w_a_out, conv_b_w, conv_b_b,
          norm_b_g, norm_b_b, w_b_out, q_norm_g, k_norm_g, w_c_out, w_o, w_ada, b_ada, ln_g, ln_b,
          w_router, router_bias, w_gate_up, w_down, table, iota, y_prompt, y_sample, new_k, new_v):
    DEPTH = w_in.shape[0]
    ALPHA = float((2 * DEPTH) ** 0.25)
    ctx = ExitStack()
    with ctx:
        def sb(name, shape, dt=F32):
            return ctx.enter_context(nc.sbuf_tensor(name, shape, dt))

        def sem(name):
            return ctx.enter_context(nc.semaphore(name))

        stage = sb("stage", [P, STAGES, 2048])
        split = sb("split", [P, SPLITS, 2, 2048], F16)
        arena = sb("arena", [P, 31336])
        tab = sb("tab", [P, 5 * 128 + 512 + 16])
        ident, mean_mat, head_mat, rot_mat, earlier_mat = (tab[:, 128 * i:128 * i + 128] for i in range(5))
        cos_t, sin_t, iota16 = tab[:, 640:896], tab[:, 896:1152], tab[:, 1152:1168]
        params = sb("params", [P, DEPTH, 8 * NPAR])
        cur = sb("cur", [P, 8, NPAR])
        mod = sb("mod", [P, 6, 8, 2])
        cond_split = sb("cond_split", [P, 2, 8, 2], F16)
        wr = sb("wr", [P, 8, 16])
        rbias = sb("rbias", [P, 16])
        qg8 = sb("qg8", [P, 1])
        eps = sb("eps", [P, 3])
        ident16 = sb("ident16", [P, P], F16)
        std = sb("std", [P, 400])
        mx = sb("mx", [P, 48])
        rsum = sb("rsum", [P, 2, 48])
        slots_i = sb("slots_i", [1, 16], I32)
        PS = ctx.enter_context(nc.psum_tensor("PS", [P, 8, 512], F32))

        def region(at, *dims, dt=F32):
            n = math.prod(dims)
            words = n if dt == F32 else n // 2
            v = arena[:, at:at + words]
            if dt != F32:
                v = v.bitcast(dt)
            if len(dims) == 2:
                v = v.rearrange("p (a b) -> p a b", a=dims[0])
            if len(dims) == 3:
                v = v.rearrange("p (a b c) -> p a b c", a=dims[0], b=dims[1])
            return v

        X = region(0, 8, 384)
        H = region(3072, 2, 8, 384, dt=F16)
        BIN = region(6144, 8, 429)
        OPB = region(6144, 2, 8, 384, dt=F16)
        BACC = region(9576, 8, 399)
        OPA = region(12768, 2, 8, 384, dt=F16)
        Q = region(15840, 8, 384)
        SQB = region(15840, 8, 399)
        OPM = region(15840, 2, 8, 384, dt=F16)
        HF = region(19032, 8, 384)
        SQQ = region(19032, 8, 384)
        OPC = region(19032, 2, 8, 384, dt=F16)
        KC = region(22104, 256)
        SQK = region(22360, 2, 384)
        RT = region(23128, 2, 384)
        ROT = region(23896, 2, 256)
        PR = region(22104, 4, 384)
        PT = region(23640, 3, 4, 128)
        M = region(22104, 8, 384)
        KT = region(25176, 2, 512)
        KTS = region(26200, 2, 512)
        V = region(27224, 4, 256)
        AIN = region(28248, 2, 387)
        ACV = region(29024, 2, 385)
        G = region(29800, 2, 384)
        KOUT = region(30568, 256)
        Y = region(30568, 2, 384)
        H2 = region(3072, 8, 384)
        SQ = region(3072, 8, 384)
        GT = region(3072, 2, 512)
        HID = region(4096, 2, 4, 512, dt=F16)
        HTOK = region(6144, 2, 3, 1024, dt=F16)
        XG = region(9216, 2, 8, 896, dt=F16)
        YSH, YSL = region(9216, 6, 1024, dt=F16), region(12288, 6, 1024, dt=F16)
        YT = region(16384, 8, 896)
        ONE = region(23552, 3, 768, dt=F16)
        ONE1 = region(24704, 3, 768, dt=F16)
        SW = region(27008, 6, 384, dt=F16)
        SIG = region(29800, 2, 2, BLK)
        HF2 = region(6144, 2, BLK)
        sel_at = [30312]

        def small(*dims):
            n = math.prod(dims)
            sel_at[0] += n
            return region(sel_at[0] - n, *dims)
        LG = region(29800, 384)[0:16]
        score, sel, selm, one1, one2, picked, key = (small(3, 16) for _ in range(7))
        pair_hi, pair_lo, grp = small(2, 3, 4), small(2, 3, 4), small(4, 3, 4)
        top = small(3)
        scan = small(4, 16)
        slot = small(3, 16)
        pick_s, pick_w = small(2, 3), small(2, 3)
        pick_split = region(sel_at[0], 4, 3, dt=F16)
        sel_at[0] += 6
        diff, wslot = small(3), small(6)
        iota768 = region(18688, 768, dt=F16)
        cond = region(16384, 3, 16)
        PROWS = region(6144, 1024)
        XTOK = region(12768, 3, 1024)
        OUT = region(12768, 3, 1024)

        landed = [sem(f"landed{i}") for i in range(STAGES)]
        hi_done = sem("hi_done")
        lo_done = sem("lo_done")
        panel_used = sem("panel_used")
        small_in, tokens_in = sem("small_in"), sem("tokens_in")
        pro_full, pro_free_act, pro_free_dve = sem("pro_full"), sem("pro_free_act"), sem("pro_free_dve")
        cond_sig, cond_ok = sem("cond_sig"), sem("cond_ok")
        tile_full, tile_act, tile_dve = sem("tile_full"), sem("tile_act"), sem("tile_dve")
        cur_ok, eps_ok = sem("cur_ok"), sem("eps_ok")
        h_f, h_hi, h_lo = sem("h_f"), sem("h_hi"), sem("h_lo")
        pads = sem("pads")
        conv_b, conv_dve = sem("conv_b"), sem("conv_dve")
        kv_in, iota_in = sem("kv_in"), sem("iota_in")
        sq_qk = sem("sq_qk")
        ck_full, ck_ok, kn_full, kn_ok, kv_out = (sem("ck_full"), sem("ck_ok"), sem("kn_full"), sem("kn_ok"),
                                                  sem("kv_out"))
        rms_full, rms_std, qk_norm = sem("rms_full"), sem("rms_std"), sem("qk_norm")
        rope_full, rope_ok, swap_ok = sem("rope_full"), sem("rope_ok"), sem("swap_ok")
        s_full, s_max, p_exp, p_norm = sem("s_full"), sem("s_max"), sem("p_exp"), sem("p_norm")
        pt_full, pt_act, pt_dve = sem("pt_full"), sem("pt_act"), sem("pt_dve")
        o_full, o_hi, o_lo = sem("o_full"), sem("o_hi"), sem("o_lo")
        opa_hi, opa_lo = sem("opa_hi"), sem("opa_lo")
        sqb, lnb_full, lnb_msq, lnb_var, lnb_std, lnb_norm, lnb_aff = (
            sem("sqb"), sem("lnb_full"), sem("lnb_msq"), sem("lnb_var"), sem("lnb_std"), sem("lnb_norm"),
            sem("lnb_aff"))
        opb_f, opb_hi, opb_lo = sem("opb_f"), sem("opb_hi"), sem("opb_lo")
        m_ok, opm_hi, opm_lo = sem("m_ok"), sem("opm_hi"), sem("opm_lo")
        z_ok = sem("z_ok")
        z_sq, ln_full, ln_msq, ln_var, ln_std, ln_norm, x_ok = (
            sem("z_sq"), sem("ln_full"), sem("ln_msq"), sem("ln_var"), sem("ln_std"), sem("ln_norm"), sem("x_ok"))
        h2_ok = sem("h2_ok")
        lg_full, lg_ok, lt_full, score_ok = sem("lg_full"), sem("lg_ok"), sem("lt_full"), sem("score_ok")
        ht_full, ht_hi, ht_lo = sem("ht_full"), sem("ht_hi"), sem("ht_lo")
        pick_ok, rank_full, slot_ok, one_ok = (sem("pick_ok"), sem("rank_full"), sem("slot_ok"),
                                               sem("one_ok"))
        xg_full, xg_hi, xg_lo, xg_pad = sem("xg_full"), sem("xg_hi"), sem("xg_lo"), sem("xg_pad")
        sw_full, sw_ok = sem("sw_full"), sem("sw_ok")
        gate_full, up_full, down_full = sem("gate_full"), sem("up_full"), sem("down_full")
        gate_sig, gate_free, up_free, down_free = sem("gate_sig"), sem("gate_free"), sem("up_free"), sem("down_free")
        ys_full, ys_act, ys_dve, f_full = sem("ys_full"), sem("ys_act"), sem("ys_dve"), sem("f_full")
        dve_step, act_step, pool_step = sem("dve_step"), sem("act_step"), sem("pool_step")
        sp_ready, pe_ready = sem("sp_ready"), sem("pe_ready")
        blk_step = sem("blk_step")
        y_full, y_act, y_out = sem("y_full"), sem("y_act"), sem("y_out")
        counts = {}

        def inc(ins, s):
            ins.then_inc(s, 1)
            counts[s.name] = counts.get(s.name, 0) + 1
            return ins

        PER = dict(tile_full=NTILE, tile_act=NT_ACT, tile_dve=NT_DVE, cur_ok=2, h_f=8, h_hi=8, h_lo=8,
                   pads=1, conv_b=POOL_CHUNKS, conv_dve=8 - POOL_CHUNKS, sq_qk=10, ck_full=1, ck_ok=1,
                   kn_full=1, kn_ok=1, rms_full=10, rms_std=10, qk_norm=10, rope_full=5, rope_ok=5, swap_ok=2,
                   s_full=48, s_max=48, p_exp=48, p_norm=48, pt_full=48, pt_act=24, pt_dve=24, o_full=12, o_hi=12,
                   o_lo=12, opa_hi=8, opa_lo=8, sqb=8, lnb_full=2, lnb_msq=1, lnb_var=1,
                   lnb_std=1, lnb_norm=1, lnb_aff=8, opb_f=8, opb_hi=8, opb_lo=8, m_ok=8, opm_hi=8, opm_lo=8,
                   z_ok=8, z_sq=16, ln_full=4, ln_msq=2, ln_var=2, ln_std=2, ln_norm=16, x_ok=16, h2_ok=8,
                   lg_full=1, lg_ok=1, lt_full=1, score_ok=1, ht_full=6, ht_hi=6, ht_lo=6, pick_ok=1, rank_full=1,
                   slot_ok=1, one_ok=3, xg_full=16, xg_hi=16, xg_lo=16, xg_pad=1, sw_full=6, sw_ok=6,
                   ys_full=12, ys_act=12, ys_dve=12, f_full=8, dve_step=DVE_STEPS, act_step=ACT_STEPS,
                   pool_step=POOL_STEPS)

        AHEAD = ("tile_dve", "z_ok", "x_ok", "o_full")

        def waiter(eng, layer):
            def wait(s, n):
                eng.wait_ge(s, layer * PER[s.name] + n + (s.name in AHEAD))
            return wait

        def stepper(eng, layer, s):
            k = [0]

            def step(ins):
                inc(ins, s)
                k[0] += 1
                eng.wait_ge(s, layer * PER[s.name] + k[0])
            return step

        def wait_z(wait, k, ch):
            if k == 0:
                wait(tile_dve, dve_count(MIX.index(("o", ch // 2)), ch % 2))
            else:
                wait(z_ok, ch + 1)

        def wait_conv(wait, ch):
            if ch < POOL_CHUNKS:
                wait(conv_b, ch + 1)
            else:
                wait(conv_dve, ch - POOL_CHUNKS + 1)

        def counter(eng, name):
            r = ctx.enter_context(eng.register(name))
            eng.reg_mov(r, 2)
            return r

        def load_slots(eng, ex):
            at = bass.ds(ex, 1) if not isinstance(ex, int) else slice(ex, ex + 1)
            return eng.value_load(slots_i[0:1, at], min_val=1, max_val=SLOT_STEP * 769)

        def unpack(eng, slots):
            why = "the table holds 512 * (0..768) + (1..384)"
            return (nc.s_assert_within(eng.snap(slots // SLOT_STEP), 0, 768, skip_runtime_bounds_check_because=why),
                    nc.s_assert_within(eng.snap(slots % SLOT_STEP), 1, 384, skip_runtime_bounds_check_because=why))

        def expert_panels(eng, held, panel):
            eng.reg_mov(held, load_slots(eng, 0))
            here = unpack(eng, eng.snap(held))
            for i, (kind, half) in enumerate(EXPERT_FIRST):
                panel(kind, half, NMIX + i, 0, 0, here)
            with eng.Fori(0, NEXP - 1) as ex:
                following = eng.snap(ex + 1)
                here = unpack(eng, eng.snap(held))
                eng.reg_mov(held, load_slots(eng, following))
                ahead = unpack(eng, eng.snap(held))
                for i, (kind, half) in enumerate(EXPERT_LOOP):
                    if kind == "down":
                        panel(kind, half, NMIX + 4 + i, ex, ex, here)
                    else:
                        panel(kind, half, NMIX + 4 + i, ex, following, ahead)
            here = unpack(eng, eng.snap(held))
            for i, (kind, half) in enumerate(EXPERT_LAST):
                panel(kind, half, NPANEL - 2 + i, 0, NEXP - 1, here)

        def two(eng, n, kind, width):
            return PS[:, bass.ds(eng.snap(n % 2 + BANK[kind]), 1), 0:width]

        def block_at(eng, start, rel):
            at = eng.snap(start + rel)
            return nc.s_assert_within(at, 0, 768, skip_runtime_bounds_check_because="slots end at 768")

        def wait_iota(eng, layer):
            eng.wait_ge(iota_in, layer * 16 + 16)

        def parameters(lay):
            r = lay * NPAR
            return [(PROWS[r:r + 31, :], conv_b_w[lay]), (PROWS[r + CONVA:r + CONVA + 3, :], conv_a_w[lay]),
                    (PROWS[r + CONVBB:r + CONVBB + 1, :], conv_b_b[lay:lay + 1]),
                    (PROWS[r + NBG:r + NBG + 1, :], norm_b_g[lay:lay + 1]),
                    (PROWS[r + NBB:r + NBB + 1, :], norm_b_b[lay:lay + 1]),
                    (PROWS[r + LNG:r + LNG + 2, :], ln_g[lay]), (PROWS[r + LNB:r + LNB + 2, :], ln_b[lay]),
                    (PROWS[r + BADA:r + BADA + 6, :], b_ada[lay].rearrange("(s n) -> s n", s=6)),
                    (PROWS[r + QG:r + QG + 1, :].rearrange("p (r d) -> p r d", d=HEAD),
                     q_norm_g[lay:lay + 1].unsqueeze(1).broadcast_to([1, 16, HEAD])),
                    (PROWS[r + KG:r + KG + 1, :].rearrange("p (r d) -> p r d", d=HEAD),
                     k_norm_g[lay:lay + 1].unsqueeze(1).broadcast_to([1, 16, HEAD]))]

        NSMALL, NTOKENS = 4 + 10 * (DEPTH - DEPTH // 2), 3 + 10 * (DEPTH // 2)
        block = ctx.enter_context(nc.Block())

        @block.sync
        def _(sp):
            def panel_source(layer, kind, j):
                cols = slice(j * PCOL, (j + 1) * PCOL)
                if kind == "ada":
                    w = w_ada
                elif kind in ("wa", "wb", "wc", "o"):
                    w = dict(wa=w_a_out, wb=w_b_out, wc=w_c_out, o=w_o)[kind]
                else:
                    w = w_in
                    cols = slice(COLS[kind] + j * PCOL, COLS[kind] + (j + 1) * PCOL)
                return w[bass.ds(layer, 1), :, cols].rearrange("l (k p) n -> p (l k) n", p=P)

            loads = []
            for lay in range(DEPTH // 2):
                loads += parameters(lay)
            loads += [(tab[:], table), (XTOK[:, 0, :], x_prompt[0]),
                      (XTOK[:, 1:3, :], x_sample[0].rearrange("(t p) n -> p t n", p=P))]
            assert len(loads) == NTOKENS
            for dst, src in loads:
                sp.dma_start(dst, src).then_inc(tokens_in, 16)
            sp.wait_ge(small_in, 16 * NSMALL)
            with sp.Fori(0, DEPTH) as layer:
                base = layer * NPANEL
                for n, (kind, j) in enumerate(MIX):
                    src = panel_source(layer, kind, j)
                    sp.wait_ge(lo_done, base + n + 1)
                    if (kind, j) == ("ab", 0):
                        sp.sem_inc(sp_ready, 1)
                    sp.dma_start(stage[:, n % STAGES, :].rearrange("p (k n) -> p k n", k=8), src
                                 ).then_inc(landed[n % STAGES], 16)

                def load(kind, half, at, loop, expert):
                    e = bass.ds(expert, 1)
                    if kind == "down":
                        src = w_down[bass.ds(layer, 1), e, :, half * 512:(half + 1) * 512]
                        k = 4
                    else:
                        c0 = half * PCOL + (512 if kind == "up" else 0)
                        src = w_gate_up[bass.ds(layer, 1), e, :, c0:c0 + PCOL]
                        k = 8
                    src = src.rearrange("l e (k p) n -> p (l e k) n", p=P)
                    sp.wait_ge(lo_done, base + 6 * loop + at + 1)
                    sp.dma_start(stage[:, at % STAGES, :].rearrange("p (k n) -> p k n", k=k), src
                                 ).then_inc(landed[at % STAGES], 16)

                for i, (kind, half) in enumerate(EXPERT_FIRST):
                    load(kind, half, NMIX + i, 0, 0)
                with sp.Fori(0, NEXP - 1) as ex:
                    for i, (kind, half) in enumerate(EXPERT_LOOP):
                        load(kind, half, NMIX + 4 + i, ex, ex if kind == "down" else sp.snap(ex + 1))
                for i, (kind, half) in enumerate(EXPERT_LAST):
                    load(kind, half, NPANEL - 2 + i, 0, NEXP - 1)

        @block.gpsimd
        def _(pool):
            with pool.Fori(0, DEPTH) as layer:
                wait = waiter(pool, layer)
                step = stepper(pool, layer, pool_step)
                for ch in range(POOL_CHUNKS):
                    wait(tile_dve, dve_count(MIX.index(("bu", ch // 2)), ch % 2))

                    def tap(out, t):
                        return pool.tensor_tensor(out, BIN[:, ch, t:t + 399],
                                                  cur[:, ch, CONVB + t:CONVB + t + 1].broadcast_to([P, 399]), ALU.mult)
                    step(tap(BACC[:, ch, :], 0))
                    for t in range(1, 31):
                        step(tap(std[:, 0:399], t))
                        step(pool.tensor_tensor(BACC[:, ch, :], BACC[:, ch, :], std[:, 0:399], ALU.add))
                    inc(pool.tensor_tensor(BACC[:, ch, :], BACC[:, ch, :],
                                           cur[:, ch, CONVBB:CONVBB + 1].broadcast_to([P, 399]), ALU.add), conv_b)

        @block.scalar
        def _(act):
            copy, sigm, square, ident_f = ACT.Copy, ACT.Sigmoid, ACT.Square, ACT.Identity
            act.preload_act_table(sigm)
            loads = [(wr[:], w_router.rearrange("(k p) e -> p k e", p=P)),
                     (rbias[:], router_bias.rearrange("(a e) -> a e", a=1).broadcast_to([P, 16])),
                     (PROWS[2 * NPAR:2 * NPAR + 1, :], c_ctx.rearrange("(a n) -> a n", a=1)),
                     (PROWS[2 * NPAR + 1:2 * NPAR + 2, :], c)]
            for lay in range(DEPTH // 2, DEPTH):
                loads += parameters(lay)
            for dst, src in loads:
                act.dma_start(dst, src).then_inc(small_in, 16)
            for s in (gate_sig, down_free, x_ok):
                act.sem_inc(s, 1 if s is x_ok else 2)
            act.wait_ge(pro_free_dve, 2)
            act.activation(cond[:, 1, :], cond[:, 0, :], sigm).then_inc(cond_sig, 1)
            for ch in range(8):
                act.wait_ge(pro_full, 3 + ch)
                act.activation(X[:, ch, :], PS[:, 4 + (2 + ch) % 4, 0:384], copy).then_inc(pro_free_act, 1)

            n_gate, n_down = counter(act, "act_gate"), counter(act, "act_down")
            held = counter(act, "act_held")
            with act.Fori(0, DEPTH) as layer:
                wait = waiter(act, layer)
                step = stepper(act, layer, act_step)
                base = layer * NPANEL

                def hi(at, ex=0):
                    act.wait_ge(landed[at % STAGES], (layer * (NPANEL // STAGES) + ex + at // STAGES + 1) * 16)
                    if SPLITS <= at < NMIX + SPLITS:
                        old = at - SPLITS
                        wait(tile_full, TILE0[old] + TILES_OF.get(MIX[old][0], 2))
                    elif at < SPLITS:
                        act.wait_ge(panel_used, layer * EXPERT_PANELS + at + 1)
                    else:
                        act.wait_ge(panel_used, layer * EXPERT_PANELS + 6 * ex + at - NMIX + 1)
                    act.activation(split[:, at % SPLITS, 0, :], stage[:, at % STAGES, :], copy,
                                   scale=WSCALE).then_inc(hi_done, 1)

                def squares(k, chunks):
                    for ch in chunks:
                        wait_z(wait, k, ch)
                        inc(act.activation(SQ[:, ch, :], X[:, ch, :], square), z_sq)

                def layer_norm(k):
                    squares(k, range(8) if k else range(6, 8))
                    act.preload_act_table(ACT.Sqrt)
                    wait(ln_full, 2 * k + 1)
                    inc(act.activation(std[:, 0:384], PS[:, 4, 0:384], square), ln_msq)
                    wait(ln_var, k + 1)
                    inc(act.activation(std[:, 0:384], std[:, 0:384], ACT.Sqrt, bias=eps[:, 0:1]), ln_std)
                    act.preload_act_table(sigm)
                    for ch in range(8):
                        wait(ln_norm, 8 * k + ch + 1)
                        inc(act.activation(X[:, ch, :], X[:, ch, :], ident_f, scale=cur[:, ch, LNG + k:LNG + k + 1],
                                           bias=cur[:, ch, LNB + k:LNB + k + 1]), x_ok)

                def evacuate(n, kind, j, i):
                    t = PS[:, (TILE0[n] + i) % NPROJ, 0:384]
                    ch = 2 * j + i
                    if kind in BY_ACT:
                        wait(tile_full, TILE0[n] + i + 1)
                    if kind in ("bg", "ga", "gc", "gb"):
                        q = ("bg", "ga", "gc", "gb").index(kind) * 4 + j
                        wait(tile_dve, dve_count(G_USERS[q - 1], i) if q else 0)
                        inc(act.activation(G[:, i, :], t, sigm, scale=UNSCALE), tile_act)
                    elif kind == "q":
                        inc(act.activation(SQQ[:, ch, :], t, square, scale=UNSCALE), sq_qk)
                        inc(act.activation(Q[:, ch, :], t, copy, scale=UNSCALE), tile_act)
                    elif kind == "k":
                        inc(act.activation(SQK[:, i, :], t, square, scale=UNSCALE), sq_qk)
                        act.activation(KT[:, i, 0:128], t[:, 0:128], copy, scale=UNSCALE)
                        inc(act.activation(KT[:, i, 256:512], t[:, 128:384], copy, scale=UNSCALE), tile_act)
                    elif kind == "v":
                        inc(act.activation(V[:, (0, 2, 3)[i], :], t[:, 0:256], copy, scale=UNSCALE), tile_act)
                    elif kind == "ac":
                        wait(pads, 1)
                        if j:
                            wait(tile_dve, dve_count(MIX.index(("ab", j - 1)), i))
                        act.activation(AIN[:, i, 1:129], t[:, 0:128], copy, scale=UNSCALE)
                        inc(act.activation(AIN[:, i, 130:386], t[:, 128:384], copy, scale=UNSCALE), tile_act)
                    elif kind == "ab":
                        wait(tile_dve, dve_count(n, i))
                        inc(act.activation(OPA[:, 0, ch, :], Y[:, i, :], copy), opa_hi)
                    elif kind == "wb":
                        wait(m_ok, ch + 1)
                        inc(act.activation(OPM[:, 0, ch, :], M[:, ch, :], copy, scale=UNSCALE), opm_hi)

                hi(0)
                hi(1)
                for n, (kind, j) in enumerate(MIX):
                    hi(n + 2)
                    b = n - ATT0
                    attend = 0 <= b < NBATCH
                    nk = 128 if b % 3 == 0 else 384
                    if (kind, j) == ("bg", 0):
                        for ch in range(8):
                            wait(h_f, ch + 1)
                            inc(act.activation(H[:, 0, ch, :], HF[:, ch, :], copy), h_hi)
                        act.dma_start(KC, cache_k[0, bass.ds(layer, 1)].rearrange("l s g d -> s (l g d)")
                                      ).then_inc(kv_in, 16)
                        act.dma_start(V[:, 1, :], cache_v[0, bass.ds(layer, 1)].rearrange("l s g d -> s (l g d)")
                                      ).then_inc(kv_in, 16)
                    if (kind, j) == ("ga", 0):
                        act.wait_ge(kv_out, layer * 32 + 32)
                    if attend:
                        for i in range(4):
                            wait(s_max, 4 * b + i + 1)
                            if b:
                                wait(pt_full, 4 * (b - 1) + i + 1)
                            inc(act.activation(PR[:, i, 0:nk], PS[:, 4 + i, 0:nk], ACT.Exp,
                                               bias=mx[:, 4 * b + i:4 * b + i + 1],
                                               accum_out=rsum[:, 0, 4 * b + i:4 * b + i + 1]), p_exp)
                    for i in range(TILES_OF.get(kind, 2)):
                        evacuate(n, kind, j, i)
                        if attend and i == 0:
                            for h in (0, 2):
                                wait(pt_full, 4 * b + h + 1)
                                wait(o_full, b)
                                inc(act.activation(PT[:, 0:nk // 128, h, :],
                                                   PS[:, 4 + h, 0:nk].rearrange("p (k q) -> p k q", q=128), copy),
                                    pt_act)
                    if attend:
                        wait(o_full, b + 1)
                        inc(act.activation(OPC[:, 0, 2 * (b // 3):2 * (b // 3) + 2, (b % 3) * 128:(b % 3 + 1) * 128],
                                           PS[:, 3, 0:256].rearrange("p (c q) -> p c q", c=2), copy), o_hi)
                    if n in RMS_AT:
                        if 0 in RMS_AT[n]:
                            wait(ck_full, 1)
                            inc(act.activation(KT[:, :, 128:256],
                                               PS[:, 3, 0:256].rearrange("p (c t) -> p c t", c=2), copy), ck_ok)
                        for i in RMS_AT[n]:
                            wait(rms_full, i + 1)
                            if i > 1:
                                wait(qk_norm, i - 1)
                            inc(act.activation(RT[:, i % 2, :], PS[:, 4 + i % 4, 0:384], ACT.Sqrt, bias=eps[:, 1:2]),
                                rms_std)
                    if 0 in ROPE_AT.get(n, ()):
                        wait(kn_full, 1)
                        inc(act.activation(KOUT, PS[:, 3, 0:256], copy), kn_ok)
                        wait(kn_ok, 1)
                        act.dma_start(new_k[0, bass.ds(layer, 1)].rearrange("l s g d -> s (l g d)"), KOUT
                                      ).then_inc(kv_out, 16)
                        wait(tile_act, act_count(MIX.index(("v", 0)), 2))
                        act.dma_start(new_v[0, bass.ds(layer, 1)].rearrange("l s g d -> s (l g d)"), V[:, 0, :]
                                      ).then_inc(kv_out, 16)
                    if 4 in ROPE_AT.get(n, ()):
                        wait(rope_ok, 5)
                        wait(ck_ok, 1)
                        inc(act.activation(KTS[64:128], KT[0:64], copy), swap_ok)
                        inc(act.activation(KTS[0:64], KT[64:128], copy), swap_ok)
                    if kind == "o" and j:
                        squares(0, range(2 * j - 2, 2 * j))
                    if n == LNB_AT:
                        for ch in range(8):
                            wait_conv(wait, ch)
                            inc(act.activation(SQB[:, ch, :], BACC[:, ch, :], square), sqb)
                    if n == LNB_AT + 2:
                        wait(lnb_full, 2)
                        inc(act.activation(std[:, 0:399], PS[:, 4, 0:399], square), lnb_msq)
                        wait(lnb_var, 1)
                        inc(act.activation(std[:, 0:399], std[:, 0:399], ACT.Sqrt, bias=eps[:, 2:3]), lnb_std)
                    if n in SILU_AT:
                        wait(lnb_norm, 1)
                        for ch in SILU_AT[n]:
                            gain, bias = cur[:, ch, NBG:NBG + 1], cur[:, ch, NBB:NBB + 1]
                            step(act.activation(SQB[:, ch, :], BACC[:, ch, :], sigm, scale=gain, bias=bias))
                            inc(act.activation(BACC[:, ch, :], BACC[:, ch, :], ident_f, scale=gain, bias=bias),
                                lnb_aff)
                        for ch in SILU_AT[n]:
                            wait(opb_f, ch + 1)
                            act.activation(OPB[:, 0, ch, 0:128], BACC[:, ch, 0:128], copy)
                            inc(act.activation(OPB[:, 0, ch, 128:384], BACC[:, ch, 143:399], copy), opb_hi)

                layer_norm(0)
                act.dma_start(iota768, iota).then_inc(iota_in, 16)
                wait(lg_full, 1)
                inc(act.activation(LG, PS[0:16, 6, 0:384], copy), lg_ok)
                wait(lt_full, 1)
                inc(act.activation(score, PS[:, 7, 0:48].rearrange("p (t e) -> p t e", t=3), sigm), score_ok)
                for i in range(6):
                    wait(ht_full, i + 1)
                    inc(act.activation(HTOK[:, 0, i // 2, (i % 2) * 512:(i % 2 + 1) * 512], PS[:, i, :], copy), ht_hi)
                for i in range(16):
                    wait(xg_full, i + 1)
                    inc(act.activation(XG[:, 0, i // 2, (i % 2) * 384:(i % 2 + 1) * 384], PS[:, i % 4, 0:384], copy),
                        xg_hi)
                for i in range(6):
                    wait(sw_full, i + 1)
                    act.activation(SW[:, i, :], PS[:, 4 + i % 4, 0:384], copy)
                    inc(act.activation(wslot[:, i:i + 1], PS[:, 4 + i % 4, 384:385], copy, scale=UNSCALE), sw_ok)

                def panel(kind, half, at, loop, expert, slots):
                    start, cnt = slots
                    if at < NPANEL - 2:
                        hi(at + 2, loop)
                    if kind == "gate":
                        with act.Fori(0, cnt, BLK):
                            n = act.snap(n_gate)
                            tile = two(act, n, kind, 2 * BLK).rearrange("p b (c s) -> p b c s", c=2)
                            sig = SIG[:, bass.ds(act.snap(n % 2), 1)]
                            before = act.snap(n - 1)
                            act.reg_add(n_gate, n_gate, 1)
                            now = act.snap(n_gate)
                            act.wait_ge(gate_free, before)
                            act.wait_ge(gate_full, now)
                            act.activation(sig, tile, sigm, scale=UNSCALE).then_inc(gate_sig, 1)
                    if kind == "down":
                        with act.Fori(0, cnt, BLK) as rel:
                            first = block_at(act, start, rel)
                            before = act.snap(n_down)
                            tile = two(act, before, kind, 4 * BLK).rearrange("p b (c s) -> p (b c) s", c=4)
                            act.reg_add(n_down, n_down, 1)
                            now = act.snap(n_down)
                            act.wait_ge(down_free, before)
                            act.wait_ge(down_full, now)
                            act.activation(YT[:, 4 * half:4 * half + 4, bass.ds(first, BLK)], tile, copy,
                                           scale=UNSCALE).then_inc(down_free, 1)

                expert_panels(act, held, panel)

                wait(sw_ok, 6)
                for i in range(12):
                    wait(ys_full, i + 1)
                    inc(act.activation(YSH[:, i // 2, (i % 2) * 512:(i % 2 + 1) * 512], PS[:, i % 8, :], copy,
                                       scale=wslot[:, i // 2:i // 2 + 1]), ys_act)
                layer_norm(1)

            for i in range(6):
                act.wait_ge(y_full, i + 1)
                act.activation(OUT[:, i // 2, (i % 2) * 512:(i % 2 + 1) * 512], PS[:, i, :], copy).then_inc(y_act, 1)
            act.wait_ge(y_act, 6)
            act.dma_start(y_prompt[0], OUT[:, 0, :]).then_inc(y_out, 16)
            act.dma_start(y_sample[0].rearrange("(t p) n -> p t n", p=P), OUT[:, 1:3, :]).then_inc(y_out, 16)
            act.wait_ge(kv_out, 32 * DEPTH)
            act.wait_ge(y_out, 32)

        @block.vector
        def _(dve):
            dve.memset(eps[:, 0:1], LN_EPS / ALPHA ** 2)
            dve.memset(eps[:, 2:3], LN_EPS)
            dve.memset(eps[:, 1:2], RMS_EPS).then_inc(eps_ok, 1)
            dve.sem_inc(lo_done, STAGES)
            for s in (gate_free, up_free, tile_dve, z_ok):
                dve.sem_inc(s, 2 if s in (gate_free, up_free) else 1)
            dve.sem_inc(blk_step, 4)
            dve.wait_ge(tokens_in, 16 * NTOKENS)
            dve.tensor_copy(ident16[:], ident)
            for half in range(2):
                dve.wait_ge(pro_full, half + 1)
                src = PS[:, 4 + half, 0:4 * (DEPTH * NPAR + 2)].rearrange("p (c r) -> p c r", c=4)
                for lay in range(DEPTH):
                    dst = params[:, lay, :].rearrange("p (c r) -> p c r", c=8)[:, 4 * half:4 * half + 4, :]
                    dve.tensor_copy(dst, src[:, :, lay * NPAR:(lay + 1) * NPAR])
                dve.tensor_copy(cond[:, 0, 8 * half:8 * half + 8].rearrange("p (c g) -> p c g", c=4),
                                src[:, :, DEPTH * NPAR:DEPTH * NPAR + 2]).then_inc(pro_free_dve, 1)
            dve.wait_ge(cond_sig, 1)
            dve.tensor_tensor(cond[:, 2, :], cond[:, 0, :], cond[:, 1, :], ALU.mult).then_inc(cond_ok, 1)
            dve.wait_ge(cond_ok, 1)
            silu = cond[:, 2, :].rearrange("p (c g) -> p c g", c=8)
            dve.tensor_copy(cond_split[:, 0], silu).then_inc(cond_ok, 1)
            dve.wait_ge(cond_ok, 2)
            dve.tensor_tensor(cond_split[:, 1], silu, cond_split[:, 0], ALU.subtract).then_inc(cond_ok, 1)

            n_gate, n_up = counter(dve, "dve_gate"), counter(dve, "dve_up")
            held = counter(dve, "dve_held")
            with dve.Fori(0, DEPTH) as layer:
                wait = waiter(dve, layer)
                step = stepper(dve, layer, dve_step)
                base = layer * NPANEL

                def lo(at, ex=0):
                    dve.wait_ge(hi_done, base + 6 * ex + at + 1)
                    dve.scalar_tensor_tensor(split[:, at % SPLITS, 1, :], stage[:, at % STAGES, :], WSCALE,
                                             split[:, at % SPLITS, 0, :], op0=ALU.mult, op1=ALU.subtract
                                             ).then_inc(lo_done, 1)

                def variance(width):
                    s = std[:, 0:width]
                    step(dve.scalar_tensor_tensor(s, s, -1.0, PS[:, 5, 0:width], op0=ALU.mult, op1=ALU.add))
                    return dve.tensor_scalar(s, s, 0.0, None, ALU.max)

                def modulated(ch):
                    wait(x_ok, ch + 1)
                    for g, cols in GRPS:
                        ins = dve.tensor_scalar(H2[:, ch, cols], X[:, ch, cols], mod[:, 4, ch, g:g + 1],
                                                mod[:, 3, ch, g:g + 1], ALU.mult, ALU.add)
                    inc(ins, h2_ok)

                def layer_norm(k):
                    wait(ln_msq, k + 1)
                    wait(ln_full, 2 * k + 2)
                    inc(variance(384), ln_var)
                    step(dve.tensor_tensor(X, X, PS[:, 4, 0:384].unsqueeze(1).broadcast_to([P, 8, 384]), ALU.subtract))
                    wait(ln_std, k + 1)
                    step(dve.reciprocal(std[:, 0:384], std[:, 0:384]))
                    for ch in range(10):
                        if ch < 8:
                            inc(dve.tensor_tensor(X[:, ch, :], X[:, ch, :], std[:, 0:384], ALU.mult), ln_norm)
                        if k == 0 and ch >= 2:
                            modulated(ch - 2)

                def evacuate(n, kind, j, i):
                    t = PS[:, (TILE0[n] + i) % NPROJ, 0:384]
                    ch = 2 * j + i
                    if kind not in BY_ACT:
                        wait(tile_full, TILE0[n] + i + 1)
                    if kind == "ada":
                        s, c0 = j // 4, 2 * (j % 4)
                        inc(dve.scalar_tensor_tensor(
                            mod[:, s, c0:c0 + 2, :], t[:, 0:4].rearrange("p (c g) -> p c g", c=2), UNSCALE,
                            cur[:, c0:c0 + 2, BADA + s:BADA + s + 1].broadcast_to([P, 2, 2]),
                            op0=ALU.mult, op1=ALU.add), tile_dve)
                        if j in (7, 11, 19, 23):
                            wait(tile_dve, dve_count(n, 0))
                        if j in (7, 19):
                            step(dve.tensor_scalar(mod[:, s], mod[:, s], 1.0, None, ALU.add))
                        if j == 11:
                            step(dve.tensor_scalar(mod[:, s], mod[:, s], UNSCALE / ALPHA, None, ALU.mult))
                        if j == 23:
                            step(dve.tensor_scalar(mod[:, s], mod[:, s], 1 / ALPHA, None, ALU.mult))
                    elif kind == "bu":
                        wait(tile_act, act_count(n - 1, i))
                        dve.scalar_tensor_tensor(BIN[:, ch, 15:143], t[:, 0:128], UNSCALE, G[:, i, 0:128],
                                                 op0=ALU.mult, op1=ALU.mult)
                        inc(dve.scalar_tensor_tensor(BIN[:, ch, 158:414], t[:, 128:384], UNSCALE, G[:, i, 128:384],
                                                     op0=ALU.mult, op1=ALU.mult), tile_dve)
                    elif kind == "ax":
                        wait(tile_act, act_count(n - 1, i))
                        dve.scalar_tensor_tensor(AIN[:, i, 1:129], t[:, 0:128], UNSCALE, AIN[:, i, 1:129],
                                                 op0=ALU.mult, op1=ALU.mult)
                        inc(dve.scalar_tensor_tensor(AIN[:, i, 130:386], t[:, 128:384], UNSCALE, AIN[:, i, 130:386],
                                                     op0=ALU.mult, op1=ALU.mult), tile_dve)
                        wait(tile_dve, dve_count(n, i))
                        step(dve.tensor_scalar(ACV[:, i, :], AIN[:, i, 0:385], cur[:, ch, CONVA:CONVA + 1], None,
                                               ALU.mult))
                        for tap in (1, 2):
                            step(dve.scalar_tensor_tensor(ACV[:, i, :], AIN[:, i, tap:tap + 385],
                                                          cur[:, ch, CONVA + tap:CONVA + tap + 1], ACV[:, i, :],
                                                          op0=ALU.mult, op1=ALU.add))
                    elif kind == "ab":
                        if j:
                            wait(opa_lo, ch - 1)
                        else:
                            dve.wait_ge(kv_out, layer * 32 + 32)
                        dve.scalar_tensor_tensor(Y[:, i, 0:128], t[:, 0:128], UNSCALE, ACV[:, i, 0:128],
                                                 op0=ALU.mult, op1=ALU.mult)
                        inc(dve.scalar_tensor_tensor(Y[:, i, 128:384], t[:, 128:384], UNSCALE, ACV[:, i, 129:385],
                                                     op0=ALU.mult, op1=ALU.mult), tile_dve)
                        wait(opa_hi, ch + 1)
                        inc(dve.tensor_tensor(OPA[:, 1, ch, :], Y[:, i, :], OPA[:, 0, ch, :], ALU.subtract), opa_lo)
                    elif kind == "wa":
                        wait(tile_act, act_count(n - 1, i))
                        inc(dve.tensor_tensor(M[:, ch, :], t, G[:, i, :], ALU.mult), tile_dve)
                    elif kind in ("wc", "wb"):
                        wait(tile_act, act_count(n - 1, i))
                        inc(dve.tensor_tensor(Y[:, i, :], t, G[:, i, :], ALU.mult), tile_dve)
                        wait(tile_dve, dve_count(n, i))
                        ins = dve.tensor_tensor(M[:, ch, :], M[:, ch, :], Y[:, i, :], ALU.add)
                        if kind == "wc":
                            step(ins)
                        else:
                            inc(ins, m_ok)
                            wait(opm_hi, ch + 1)
                            inc(dve.scalar_tensor_tensor(OPM[:, 1, ch, :], M[:, ch, :], UNSCALE, OPM[:, 0, ch, :],
                                                         op0=ALU.mult, op1=ALU.subtract), opm_lo)
                    elif kind == "o":
                        for g, cols in GRPS:
                            ins = dve.scalar_tensor_tensor(X[:, ch, cols], t[:, cols], mod[:, 2, ch, g:g + 1],
                                                           X[:, ch, cols], op0=ALU.mult, op1=ALU.add)
                        inc(ins, tile_dve)

                wait(x_ok, 0)
                inc(dve.tensor_copy(cur[:].rearrange("p c r -> p (c r)"), params[:, bass.ds(layer, 1), :].rearrange(
                    "p l n -> p (l n)")), cur_ok)
                wait(cur_ok, 1)
                inc(dve.tensor_scalar(qg8[:], cur[:, 0, QG:QG + 1], HEAD ** -0.5, None, ALU.mult), cur_ok)
                lo(0)
                lo(1)
                for n, (kind, j) in enumerate(MIX):
                    lo(n + 2)
                    b = n - ATT0
                    attend = 0 <= b < NBATCH
                    nk = 128 if b % 3 == 0 else 384
                    if attend:
                        for i in range(4):
                            wait(s_full, 4 * b + i + 1)
                            inc(dve.tensor_reduce(mx[:, 4 * b + i:4 * b + i + 1], PS[:, 4 + i, 0:nk], AX.X, ALU.max,
                                                  negate=True), s_max)
                        for i in range(4):
                            at = slice(4 * b + i, 4 * b + i + 1)
                            wait(p_exp, 4 * b + i + 1)
                            step(dve.reciprocal(rsum[:, 1, at], rsum[:, 0, at]))
                            inc(dve.tensor_scalar(PR[:, i, 0:nk], PR[:, i, 0:nk], rsum[:, 1, at], None, ALU.mult),
                                p_norm)
                    for i in range(TILES_OF.get(kind, 2)):
                        evacuate(n, kind, j, i)
                        if attend and i == 0:
                            for h in (1, 3):
                                wait(pt_full, 4 * b + h + 1)
                                wait(o_full, b)
                                inc(dve.tensor_copy(PT[:, 0:nk // 128, h, :],
                                                    PS[:, 4 + h, 0:nk].rearrange("p (k q) -> p k q", q=128)), pt_dve)
                    if attend:
                        wait(o_hi, b + 1)
                        at = (slice(2 * (b // 3), 2 * (b // 3) + 2), slice((b % 3) * 128, (b % 3 + 1) * 128))
                        inc(dve.tensor_tensor(OPC[:, 1, at[0], at[1]], PS[:, 3, 0:256].rearrange("p (c q) -> p c q", c=2),
                                              OPC[:, 0, at[0], at[1]], ALU.subtract), o_lo)
                    for ch, tap in CONV_TAPS.get(n, ()):
                        if tap == 0:
                            wait(tile_dve, dve_count(MIX.index(("bu", ch // 2)), ch % 2))
                            step(dve.tensor_scalar(BACC[:, ch, :], BIN[:, ch, 0:399], cur[:, ch, CONVB:CONVB + 1],
                                                   cur[:, ch, CONVBB:CONVBB + 1], ALU.mult, ALU.add))
                            continue
                        ins = dve.scalar_tensor_tensor(BACC[:, ch, :], BIN[:, ch, tap:tap + 399],
                                                       cur[:, ch, CONVB + tap:CONVB + tap + 1], BACC[:, ch, :],
                                                       op0=ALU.mult, op1=ALU.add)
                        if tap < 30:
                            step(ins)
                        else:
                            inc(ins, conv_dve)
                    if (kind, j) == ("ada", 7):
                        for at in (slice(0, 15), slice(143, 158), slice(414, 429)):
                            dve.memset(BIN[:, :, at], 0.0)
                        for at in (slice(0, 1), slice(129, 130), slice(386, 387)):
                            ins = dve.memset(AIN[:, :, at], 0.0)
                        inc(ins, pads)
                        wait(pads, 1)
                        for ch in range(9):
                            if ch < 8:
                                for g, cols in GRPS:
                                    ins = dve.tensor_scalar(HF[:, ch, cols], X[:, ch, cols], mod[:, 1, ch, g:g + 1],
                                                            mod[:, 0, ch, g:g + 1], ALU.mult, ALU.add)
                                inc(ins, h_f)
                            if ch > 0:
                                wait(h_hi, ch)
                                inc(dve.tensor_tensor(H[:, 1, ch - 1, :], HF[:, ch - 1, :], H[:, 0, ch - 1, :],
                                                      ALU.subtract), h_lo)
                    if n in RMS_AT:
                        for i in RMS_AT[n]:
                            r = RT[:, i % 2, :]
                            wait(rms_std, i + 1)
                            step(dve.reciprocal(r, r))
                            if i < 8:
                                inc(dve.scalar_tensor_tensor(Q[:, i, :], Q[:, i, :], qg8[:, 0:1], r, op0=ALU.mult,
                                                             op1=ALU.mult), qk_norm)
                            else:
                                for k_at, r_at in ((slice(0, 128), slice(0, 128)), (slice(256, 512), slice(128, 384))):
                                    ins = dve.scalar_tensor_tensor(KT[:, i - 8, k_at], KT[:, i - 8, k_at],
                                                                   cur[:, 0, KG:KG + 1], r[:, r_at], op0=ALU.mult,
                                                                   op1=ALU.mult)
                                inc(ins, qk_norm)
                    if n in ROPE_AT:
                        cos2 = cos_t.unsqueeze(1).broadcast_to([P, 2, 256])
                        sin2 = sin_t.unsqueeze(1).broadcast_to([P, 2, 256])
                        for pr in ROPE_AT[n]:
                            v = Q[:, 2 * pr:2 * pr + 2, 128:384] if pr < 4 else KT[:, :, 256:512]
                            wait(rope_full, pr + 1)
                            step(dve.tensor_tensor(ROT, PS[:, 4 + pr % 4, :].rearrange("p (c t) -> p c t", c=2), sin2,
                                                   ALU.mult))
                            step(dve.tensor_tensor(v, v, cos2, ALU.mult))
                            inc(dve.tensor_tensor(v, v, ROT, ALU.add), rope_ok)
                            wait(rope_ok, pr + 1)
                    if n == LNB_AT + 2:
                        wait(lnb_msq, 1)
                        inc(variance(399), lnb_var)
                        wait(lnb_std, 1)
                        step(dve.reciprocal(std[:, 0:399], std[:, 0:399]))
                    if n == MIX.index(("wc", 2)):
                        step(dve.tensor_tensor(BACC, BACC, PS[:, 4, 0:399].unsqueeze(1).broadcast_to([P, 8, 399]),
                                               ALU.subtract))
                    if n == MIX.index(("gc", 3)):
                        inc(dve.tensor_tensor(BACC, BACC, std[:, 0:399].unsqueeze(1).broadcast_to([P, 8, 399]),
                                              ALU.mult), lnb_norm)
                    if n in SILU_AT:
                        for ch in SILU_AT[n]:
                            wait(lnb_aff, ch + 1)
                            inc(dve.tensor_tensor(BACC[:, ch, :], BACC[:, ch, :], SQB[:, ch, :], ALU.mult), opb_f)
                        for ch in SILU_AT[n]:
                            wait(opb_hi, ch + 1)
                            dve.tensor_tensor(OPB[:, 1, ch, 0:128], BACC[:, ch, 0:128], OPB[:, 0, ch, 0:128],
                                              ALU.subtract)
                            inc(dve.tensor_tensor(OPB[:, 1, ch, 128:384], BACC[:, ch, 143:399], OPB[:, 0, ch, 128:384],
                                                  ALU.subtract), opb_lo)

                layer_norm(0)
                def first_of_max(x, out, n):
                    k = key[:, :, 0:n]
                    step(dve.tensor_reduce(top, x, AX.X, ALU.max))
                    step(dve.tensor_tensor(k, x, top.unsqueeze(2).broadcast_to([P, 3, n]), ALU.is_equal))
                    step(dve.scalar_tensor_tensor(k, k, -32.0, iota16[:, 0:n].unsqueeze(1).broadcast_to([P, 3, n]),
                                                  op0=ALU.mult, op1=ALU.add))
                    step(dve.tensor_reduce(top, k, AX.X, ALU.min))
                    step(dve.tensor_tensor(out, k, top.unsqueeze(2).broadcast_to([P, 3, n]), ALU.is_equal))

                inc(dve.memset(XG[:, :, :, 768:896], 0.0), xg_pad)
                wait(score_ok, 1)
                step(dve.tensor_tensor(sel, score, rbias[:].unsqueeze(1).broadcast_to([P, 3, 16]), ALU.add))
                four = sel.rearrange("p t (g e) -> p t g e", g=4)
                for h in range(2):
                    step(dve.tensor_tensor(pair_hi[:, h], four[:, :, :, 2 * h], four[:, :, :, 2 * h + 1], ALU.max))
                    step(dve.tensor_tensor(pair_lo[:, h], four[:, :, :, 2 * h], four[:, :, :, 2 * h + 1], ALU.min))
                step(dve.tensor_tensor(grp[:, 0], pair_hi[:, 0], pair_hi[:, 1], ALU.max))
                step(dve.tensor_tensor(grp[:, 1], pair_hi[:, 0], pair_hi[:, 1], ALU.min))
                step(dve.tensor_tensor(grp[:, 2], pair_lo[:, 0], pair_lo[:, 1], ALU.max))
                step(dve.tensor_tensor(grp[:, 1], grp[:, 1], grp[:, 2], ALU.max))
                step(dve.tensor_tensor(grp[:, 0], grp[:, 0], grp[:, 1], ALU.add))
                first_of_max(grp[:, 0], grp[:, 3], 4)
                step(dve.tensor_scalar(grp[:, 3], grp[:, 3], 1e30, -1e30, ALU.mult, ALU.add))
                step(dve.tensor_tensor(selm.rearrange("p t (g e) -> p t g e", g=4), four,
                                       grp[:, 3].unsqueeze(3).broadcast_to([P, 3, 4, 4]), ALU.add))
                first_of_max(selm, one1, 16)
                step(dve.scalar_tensor_tensor(selm, one1, -3e30, selm, op0=ALU.mult, op1=ALU.add))
                first_of_max(selm, one2, 16)
                inc(dve.tensor_tensor(picked, one1, one2, ALU.add), pick_ok)
                for h, one in enumerate((one1, one2)):
                    step(dve.tensor_tensor(sel, one, score, ALU.mult))
                    step(dve.tensor_reduce(pick_w[:, h], sel, AX.X, ALU.add))
                step(dve.tensor_tensor(top, pick_w[:, 0], pick_w[:, 1], ALU.add))
                step(dve.reciprocal(top, top))
                for h in range(2):
                    step(dve.tensor_tensor(pick_w[:, h], pick_w[:, h], top, ALU.mult))
                step(dve.tensor_tensor(diff, pick_w[:, 0], pick_w[:, 1], ALU.subtract))
                for h, part in enumerate((diff, pick_w[:, 1])):
                    step(dve.tensor_scalar(pick_split[:, 2 * h], part, WSCALE, None, ALU.mult))
                    dve.scalar_tensor_tensor(pick_split[:, 2 * h + 1], part, WSCALE, pick_split[:, 2 * h],
                                             op0=ALU.mult, op1=ALU.subtract)
                for i in range(6):
                    wait(ht_hi, i + 1)
                    at = slice((i % 2) * 512, (i % 2 + 1) * 512)
                    inc(dve.tensor_tensor(HTOK[:, 1, i // 2, at], PS[:, i, :], HTOK[:, 0, i // 2, at], ALU.subtract),
                        ht_lo)
                wait(rank_full, 1)
                step(dve.tensor_scalar(scan[:, 0], PS[:, 6, 48:64], 1024.0, None, ALU.mult))
                step(dve.tensor_copy(scan[:, 1], scan[:, 0]))
                a = 1
                for s in (1, 2, 4, 8):
                    dve.tensor_copy(scan[:, 3 - a, 0:s], scan[:, a, 0:s])
                    step(dve.tensor_tensor(scan[:, 3 - a, s:16], scan[:, a, s:16], scan[:, a, 0:16 - s], ALU.add))
                    a = 3 - a
                step(dve.tensor_tensor(scan[:, 3], scan[:, a], scan[:, 0], ALU.subtract))
                step(dve.scalar_tensor_tensor(slot, PS[:, 6, 0:48].rearrange("p (t e) -> p t e", t=3), 1024.0,
                                              scan[:, 3].unsqueeze(1).broadcast_to([P, 3, 16]), op0=ALU.mult,
                                              op1=ALU.add))
                for h, one in enumerate((one1, one2)):
                    step(dve.tensor_tensor(sel, one, slot, ALU.mult))
                    step(dve.tensor_reduce(pick_s[:, h], sel, AX.X, ALU.add))
                step(dve.tensor_scalar(scan[0:1, 0], scan[0:1, 0], 1.0, None, ALU.max))
                inc(dve.scalar_tensor_tensor(slots_i[0:1, :], scan[0:1, 3], float(SLOT_STEP), scan[0:1, 0],
                                             op0=ALU.mult, op1=ALU.add), slot_ok)
                wait_iota(dve, layer)
                for t in range(3):
                    step(dve.tensor_scalar(ONE1[:, t, :], iota768, pick_s[:, 0, t:t + 1], None, ALU.is_equal))
                    inc(dve.scalar_tensor_tensor(ONE[:, t, :], iota768, pick_s[:, 1, t:t + 1], ONE1[:, t, :],
                                                 op0=ALU.is_equal, op1=ALU.add), one_ok)
                for i in range(16):
                    at = slice((i % 2) * 384, (i % 2 + 1) * 384)
                    wait(xg_hi, i + 1)
                    inc(dve.tensor_tensor(XG[:, 1, i // 2, at], PS[:, i % 4, 0:384], XG[:, 0, i // 2, at],
                                          ALU.subtract), xg_lo)

                def panel(kind, half, at, loop, expert, slots):
                    cnt = slots[1]
                    if at < NPANEL - 2:
                        lo(at + 2, loop)
                    if kind == "gate":
                        with dve.Fori(0, cnt, BLK) as rel:
                            n = dve.snap(n_gate)
                            tile = two(dve, n, kind, 2 * BLK).rearrange("p b (c s) -> p (b c) s", c=2)
                            sig = SIG[:, bass.ds(dve.snap(n % 2), 1)].rearrange("p b c s -> p (b c) s")
                            dve.reg_add(n_gate, n_gate, 1)
                            now = dve.snap(n_gate)
                            dve.wait_ge(gate_sig, now)
                            dve.scalar_tensor_tensor(GT[:, :, bass.ds(rel, BLK)], tile, UNSCALE, sig, op0=ALU.mult,
                                                     op1=ALU.mult).then_inc(gate_free, 1)
                    if kind == "up":
                        with dve.Fori(0, cnt, BLK) as rel:
                            silus, before = dve.snap(n_gate), dve.snap(n_up)
                            tile = two(dve, before, kind, 2 * BLK).rearrange("p b (c s) -> p (b c) s", c=2)
                            done = dve.snap(n_up) * 2
                            dve.reg_add(n_up, n_up, 1)
                            now = dve.snap(n_up)
                            dve.wait_ge(gate_free, silus)
                            dve.wait_ge(up_free, before)
                            dve.wait_ge(up_full, now)
                            hid = [HID[:, s, 2 * half:2 * half + 2, bass.ds(rel, BLK)] for s in range(2)]
                            dve.scalar_tensor_tensor(HF2, tile, UNSCALE, GT[:, :, bass.ds(rel, BLK)], op0=ALU.mult,
                                                     op1=ALU.mult).then_inc(blk_step, 1)
                            dve.wait_ge(blk_step, done + 1)
                            dve.tensor_copy(hid[0], HF2).then_inc(blk_step, 1)
                            dve.wait_ge(blk_step, done + 2)
                            dve.tensor_tensor(hid[1], HF2, hid[0], ALU.subtract).then_inc(up_free, 1)

                expert_panels(dve, held, panel)

                for i in range(12):
                    wait(ys_act, i + 1)
                    at = slice((i % 2) * 512, (i % 2 + 1) * 512)
                    inc(dve.scalar_tensor_tensor(YSL[:, i // 2, at], PS[:, i % 8, :], wslot[:, i // 2:i // 2 + 1],
                                                 YSH[:, i // 2, at], op0=ALU.mult, op1=ALU.subtract), ys_dve)
                for ch in range(8):
                    wait(f_full, ch + 1)
                    for g, cols in GRPS:
                        ins = dve.scalar_tensor_tensor(X[:, ch, cols], PS[:, ch % 4, cols], mod[:, 5, ch, g:g + 1],
                                                       X[:, ch, cols], op0=ALU.mult, op1=ALU.add)
                    inc(ins, z_ok)
                layer_norm(1)

        @block.tensor
        def _(pe):
            pe.sem_inc(panel_used, SPLITS)
            for s in (gate_full, up_full, down_full):
                pe.sem_inc(s, 2)
            pe.sem_inc(o_full, 1)
            pe.wait_ge(tokens_in, 16 * NTOKENS)
            pe.wait_ge(small_in, 16 * NSMALL)
            rows = DEPTH * NPAR + 2
            for ch in range(8):
                ins = pe.transpose(PS[:, 4 + ch // 4, (ch % 4) * rows:(ch % 4 + 1) * rows],
                                   PROWS[0:rows, ch * P:(ch + 1) * P], ident[0:rows, 0:rows])
                if ch % 4 == 3:
                    ins.then_inc(pro_full, 1)
            for ch in range(8):
                q = 2 + ch
                if q in (4, 5):
                    pe.wait_ge(pro_free_dve, q - 3)
                if q > 5:
                    pe.wait_ge(pro_free_act, q - 5)
                for t in range(3):
                    ins = pe.transpose(PS[:, 4 + q % 4, t * P:(t + 1) * P], XTOK[:, t, ch * P:(ch + 1) * P], ident)
                ins.then_inc(pro_full, 1)
            pe.wait_ge(cond_ok, 3)

            n_gate, n_up, n_down, held = (counter(pe, f"pe_{x}") for x in ("gate", "up", "down", "held"))
            with pe.Fori(0, DEPTH) as layer:
                wait = waiter(pe, layer)
                base = layer * NPANEL

                def products(out, pairs):
                    for x, (lhsT, rhs) in enumerate(pairs):
                        ins = pe.matmul(out, lhsT, rhs, start=(x == 0), stop=(x == len(pairs) - 1))
                    return ins

                def weights(at, k):
                    return [split[:, at % SPLITS, s, :].rearrange("p (k n) -> p k n", k=k) for s in range(2)]

                def three(w, x, chunks, cols):
                    out = []
                    for k in range(chunks):
                        out += [(w[0][:, k, cols], x(0, k)), (w[0][:, k, cols], x(1, k)), (w[1][:, k, cols], x(0, k))]
                    return out

                operand = dict(wa=OPA, wb=OPB, wc=OPC, o=OPM)
                ready = dict(bg=h_lo, wa=opa_lo, wb=opb_lo, o=opm_lo)

                def project(n, kind, j, i):
                    q = TILE0[n] + i
                    if q >= NPROJ:
                        act = TILE_KIND[q - NPROJ] in BY_ACT
                        wait(tile_act if act else tile_dve, tiles_freed(q - NPROJ + 1, act))
                    else:
                        wait(z_ok, 0)
                    bank = PS[:, q % NPROJ, :]
                    w = weights(n, 8)
                    x = operand.get(kind, H)
                    if kind == "ada":
                        for cc in range(2):
                            ins = products(bank[:, 2 * cc:2 * cc + 2],
                                           three(w, lambda s, k: cond_split[:, s, k, :], 8, slice(cc * P, (cc + 1) * P)))
                    elif kind == "v":
                        tok = slice(i * P, (i + 1) * P)
                        pairs = []
                        for k in range(8):
                            pairs += [(H[:, 0, k, tok], w[0][:, k, :]), (H[:, 0, k, tok], w[1][:, k, :]),
                                      (H[:, 1, k, tok], w[0][:, k, :])]
                        ins = products(bank[:, 0:256], pairs)
                    else:
                        if (kind, j, i) == ("wc", 0, 0):
                            wait(o_lo, 12)
                        pairs = three(w, lambda s, k: x[:, s, k, :], 8, slice(i * P, (i + 1) * P))
                        if kind in ready and j == i == 0:
                            for m, (lhsT, rhs) in enumerate(pairs):
                                if m % 3 == 0:
                                    wait(ready[kind], m // 3 + 1)
                                ins = pe.matmul(bank[:, 0:384], lhsT, rhs, start=(m == 0), stop=(m == len(pairs) - 1))
                        else:
                            ins = products(bank[:, 0:384], pairs)
                    return ins

                def row_stats(k, source, squares, ready, sq_ready, full, width):
                    for ch in range(8):
                        ready(ch)
                        ins = pe.matmul(PS[:, 4, 0:width], mean_mat, source[:, ch, :], start=(ch == 0), stop=(ch == 7))
                    inc(ins, full)
                    for ch in range(8):
                        sq_ready(ch)
                        ins = pe.matmul(PS[:, 5, 0:width], mean_mat, squares[:, ch, :], start=(ch == 0), stop=(ch == 7))
                    inc(ins, full)

                def stats(k, ch):
                    wait_z(wait, k, ch)
                    ins = pe.matmul(PS[:, 4, 0:384], mean_mat, X[:, ch, :], start=(ch == 0), stop=(ch == 7))
                    if ch == 7:
                        inc(ins, ln_full)
                    wait(z_sq, 8 * k + ch + 1)
                    ins = pe.matmul(PS[:, 5, 0:384], mean_mat, SQ[:, ch, :], start=(ch == 0), stop=(ch == 7))
                    if ch == 7:
                        inc(ins, ln_full)

                for n, (kind, j) in enumerate(MIX):
                    b = n - ATT0
                    attend = 0 <= b < NBATCH
                    g, t = b // 3, b % 3
                    nk = 128 if t == 0 else 384
                    keys = slice(0, 128) if t == 0 else slice(128, 512)
                    if attend:
                        for i in range(4):
                            if b == 0:
                                wait(rope_ok, 5)
                                wait(swap_ok, 2)
                            else:
                                wait((pt_act, pt_dve)[i % 2], 2 * (b - 1) + i // 2 + 1)
                            rows_of = slice(64 * (i % 2), 64 * (i % 2) + 64)
                            kt = KT if g % 2 == i % 2 else KTS
                            inc(pe.matmul(PS[:, 4 + i, 0:nk], Q[rows_of, 2 * g + i // 2, t * P:(t + 1) * P],
                                          kt[rows_of, g // 2, keys], start=True, stop=True), s_full)
                    if n == LNB_AT + 2:
                        row_stats(0, BACC, SQB, lambda ch: wait_conv(wait, ch), lambda ch: wait(sqb, ch + 1),
                                  lnb_full, 399)
                    pe.wait_ge(lo_done, STAGES + base + n + 1)
                    tiles = TILES_OF.get(kind, 2)
                    for i in range(tiles):
                        ins = project(n, kind, j, i)
                        inc(ins, tile_full)
                        if attend and i == 0:
                            for h in range(4):
                                wait(p_norm, 4 * b + h + 1)
                                for kt in range(nk // P):
                                    ins = pe.transpose(PS[:, 4 + h, kt * P:(kt + 1) * P], PR[:, h, kt * P:(kt + 1) * P],
                                                       ident)
                                inc(ins, pt_full)
                    if attend:
                        wait(pt_act, 2 * b + 2)
                        wait(pt_dve, 2 * b + 2)
                        if b == 0:
                            wait(kn_ok, 1)
                        else:
                            wait(o_lo, b)
                        for half in range(2):
                            for kt in range(nk // P):
                                ins = pe.matmul(PS[64 * half:64 * half + 64, 3, 0:256],
                                                V[:, 0 if t == 0 else 1 + kt, 64 * g:64 * g + 64],
                                                PT[:, kt, half::2, :], start=(kt == 0), stop=(kt == nk // P - 1))
                        inc(ins, o_full)
                    if kind == "o" and j:
                        stats(0, 2 * j - 2)
                        stats(0, 2 * j - 1)
                    if n in RMS_AT:
                        if 0 in RMS_AT[n]:
                            pe.wait_ge(kv_in, layer * 32 + 32)
                            for ch in range(2):
                                ins = pe.transpose(PS[:, 3, ch * P:(ch + 1) * P], KC[:, ch * P:(ch + 1) * P], ident)
                            inc(ins, ck_full)
                        for i in RMS_AT[n]:
                            wait(sq_qk, i + 1)
                            if i >= 4:
                                wait(rms_std, i - 3)
                            inc(pe.matmul(PS[:, 4 + i % 4, 0:384], head_mat, SQQ[:, i, :] if i < 8 else SQK[:, i - 8, :],
                                          start=True, stop=True), rms_full)
                    if n in ROPE_AT:
                        if 0 in ROPE_AT[n]:
                            wait(qk_norm, 10)
                            wait(ck_ok, 1)
                            for ch in range(2):
                                ins = pe.transpose(PS[:, 3, ch * P:(ch + 1) * P], KT[:, ch, 0:P], ident)
                            inc(ins, kn_full)
                        for pr in ROPE_AT[n]:
                            if pr == 4:
                                wait(rope_ok, 1)
                            for x in range(2):
                                v = Q[:, 2 * pr + x, 128:384] if pr < 4 else KT[:, x, 256:512]
                                ins = pe.matmul(PS[:, 4 + pr % 4, x * 256:(x + 1) * 256], rot_mat, v, start=True,
                                                stop=True)
                            inc(ins, rope_full)

                stats(0, 6)
                stats(0, 7)
                for k in range(8):
                    wait(h2_ok, k + 1)
                    ins = pe.matmul(PS[0:16, 6, 0:384], wr[:, k, :], H2[:, k, :], start=(k == 0), stop=(k == 7))
                inc(ins, lg_full)
                wait(lg_ok, 1)
                for t in range(3):
                    ins = pe.matmul(PS[:, 7, 16 * t:16 * t + 16], LG[:, t * P:(t + 1) * P], ident[0:16, 0:16],
                                    start=True, stop=True)
                inc(ins, lt_full)
                for i in range(6):
                    for cc in range(4):
                        ins = pe.transpose(PS[:, i, cc * P:(cc + 1) * P],
                                           H2[:, 4 * (i % 2) + cc, (i // 2) * P:(i // 2 + 1) * P], ident)
                    inc(ins, ht_full)
                wait(pick_ok, 1)
                for t in range(3):
                    pairs = [(earlier_mat, picked[:, t, :])] + [(mean_mat, picked[:, u, :]) for u in range(t)]
                    products(PS[:, 6, 16 * t:16 * t + 16], pairs)
                inc(products(PS[:, 6, 48:64], [(mean_mat, picked[:, t, :]) for t in range(3)]), rank_full)
                wait(one_ok, 3)
                wait(ht_lo, 6)
                for i in range(16):
                    if i >= 4:
                        wait(xg_lo, i - 3)
                    ch, at = i // 2, slice((i % 2) * 384, (i % 2 + 1) * 384)
                    inc(products(PS[:, i % 4, 0:384], [(HTOK[:, s, t, ch * P:(ch + 1) * P], ONE[:, t, at])
                                                       for t in range(3) for s in range(2)]), xg_full)
                wait(xg_lo, 16)
                wait(xg_pad, 1)
                for i in range(6):
                    if i >= 4:
                        wait(sw_ok, i - 3)
                    blk = slice(i * P, (i + 1) * P)
                    for t in range(3):
                        pe.matmul(PS[:, 4 + i % 4, t * P:(t + 1) * P], ONE[:, t, blk], ident16[:], start=True,
                                  stop=True)
                    inc(products(PS[:, 4 + i % 4, 384:385], [(one[:, t, blk], pick_split[:, 2 * h + s, t:t + 1])
                                                             for h, one in enumerate((ONE1, ONE))
                                                             for t in range(3) for s in range(2)]), sw_full)
                wait(sw_ok, 6)
                pe.sem_inc(pe_ready, 1)

                def panel(kind, half, at, loop, expert, slots):
                    start, cnt = slots
                    w = weights(at, 4 if kind == "down" else 8)
                    with pe.Fori(0, cnt, BLK) as rel:
                        r = dict(gate=n_gate, up=n_up, down=n_down)[kind]
                        n, hidden = pe.snap(r), pe.snap(n_up)
                        tile = PS[:, bass.ds(pe.snap(n % 2 + BANK[kind]), 1), :].rearrange("p b n -> p (b n)")
                        before = pe.snap(n - 1)
                        pe.wait_ge(lo_done, STAGES + base + 6 * loop + at + 1)
                        pe.wait_ge(dict(gate=gate_free, up=up_free, down=down_free)[kind], before)
                        if kind == "down":
                            pe.wait_ge(up_free, hidden)
                            hid = HID[:, :, :, bass.ds(rel, BLK)]
                            for cc in range(4):
                                ins = products(tile[:, cc * BLK:(cc + 1) * BLK],
                                               three(w, lambda s, k: hid[:, s, k, :], 4,
                                                     slice(cc * P, (cc + 1) * P)))
                            ins.then_inc(down_full, 1)
                        else:
                            first = block_at(pe, start, rel)
                            xs = XG[:, :, :, bass.ds(first, BLK)]
                            for cc in range(2):
                                ins = products(tile[:, cc * BLK:(cc + 1) * BLK],
                                               three(w, lambda s, k: xs[:, s, k, :], 8,
                                                     slice(cc * P, (cc + 1) * P)))
                            ins.then_inc(gate_full if kind == "gate" else up_full, 1)
                        pe.reg_add(r, r, 1)
                    pe.matmul(PS[:, 3, 0:4], w[0][:, 0, 0:P], XG[:, 0, 0, 0:4], start=True, stop=True
                              ).then_inc(panel_used, 1)

                expert_panels(pe, held, panel)

                pe.wait_ge(down_free, pe.snap(n_down))
                for i in range(12):
                    if i >= 8:
                        wait(ys_dve, i - 7)
                    for cc in range(4):
                        ins = pe.transpose(PS[:, i % 8, cc * P:(cc + 1) * P],
                                           YT[:, 4 * (i % 2) + cc, (i // 2) * P:(i // 2 + 1) * P], ident)
                    inc(ins, ys_full)
                wait(ys_dve, 12)
                for ch in range(10):
                    if 4 <= ch < 8:
                        wait(z_ok, ch - 3)
                    if ch < 8:
                        inc(products(PS[:, ch % 4, 0:384], [(ys[:, s, ch * P:(ch + 1) * P], SW[:, s, :])
                                                            for s in range(6) for ys in (YSH, YSL)]), f_full)
                    if ch >= 2:
                        stats(1, ch - 2)

            pe.wait_ge(x_ok, 16 * DEPTH + 1)
            for i in range(6):
                for cc in range(4):
                    ins = pe.transpose(PS[:, i, cc * P:(cc + 1) * P],
                                       X[:, 4 * (i % 2) + cc, (i // 2) * P:(i // 2 + 1) * P], ident)
                ins.then_inc(y_full, 1)

        off = {k: (v, counts.get(k, 0)) for k, v in PER.items() if counts.get(k, 0) != v}
        assert not off, f"signals per layer (stated, emitted): {off}"


_INS = ["x_prompt", "x_sample", "c", "c_ctx", "cache_k", "cache_v", "w_in", "conv_a_w", "w_a_out", "conv_b_w",
        "conv_b_b", "norm_b_g", "norm_b_b", "w_b_out", "q_norm_g", "k_norm_g", "w_c_out", "w_o", "w_ada", "b_ada",
        "ln_g", "ln_b", "w_router", "router_bias", "w_gate_up", "w_down"]


def kernel(**inputs):
    import concourse.bacc as bacc
    from concourse.bass_utils import run_bass_kernel_spmd

    nc = bacc.Bacc("TRN2", target_bir_lowering=False, num_devices=1)
    table, iota = shape_constants()
    arrays, args = {}, {}
    for name in _INS + ["table", "iota"]:
        a = np.ascontiguousarray(inputs[name]) if name in inputs else dict(table=table, iota=iota)[name]
        arrays[f"in_{name}"] = a
        args[name] = nc.dram_tensor(f"in_{name}", a.shape, mybir.dt.from_np(a.dtype), kind="ExternalInput").ap()
    depth = arrays["in_w_in"].shape[0]
    outs = [("y_prompt", arrays["in_x_prompt"].shape), ("y_sample", arrays["in_x_sample"].shape),
            ("new_k", (1, depth, 128, 4, 64)), ("new_v", (1, depth, 128, 4, 64))]
    for name, shape in outs:
        args[name] = nc.dram_tensor(name, shape, F32, kind="ExternalOutput").ap()
    build(nc, **args)
    r = run_bass_kernel_spmd(nc, [arrays], core_ids=[0])
    return tuple(r.results[0][name] for name, _ in outs)
```
